# Optimizing a Trainium2 kernel written in Bass

```python
import jax, jax.numpy as jnp
from jax import lax
import numpy as np
import math

D_MODEL = 1024
BATCH = 1
SEQ = 512
DEPTH = 1

M_HEADS = 4
M_V_DIM = 128
M_QK_DIM = 64
M_CHUNK = 64
A_HEADS = 8
A_HEAD_DIM = 64
WINDOWS = (128, 512, 2048)
DILATIONS = (1, 4, 16)
ROT_DIM = A_HEAD_DIM // 4
ROPE_THETA = 500000.0
MIX_WIDTH = M_HEADS * M_V_DIM + A_HEADS * A_HEAD_DIM
IN_SPLITS = (M_HEADS * M_QK_DIM, M_HEADS * M_QK_DIM, M_HEADS * M_V_DIM, M_HEADS * M_V_DIM,
             4 * M_HEADS, A_HEADS * A_HEAD_DIM, A_HEADS * A_HEAD_DIM, A_HEADS * A_HEAD_DIM)
IN_COLS = sum(IN_SPLITS)
D_FF = 2816
N_MOD = 9
HALF_STEP = 0.5
EPS = 1e-6
NEG_INF = -1e30


def rms_norm(x, g):
    xf = x.astype(jnp.float32)
    y = xf * lax.rsqrt(jnp.mean(xf * xf, axis=-1, keepdims=True) + EPS)
    return (y * g.astype(jnp.float32)).astype(x.dtype)

def modulate(h, shift, scale):
    return h * (1.0 + scale) + shift

def swiglu(h, w_gu, w_down):
    g, u = jnp.split(h @ w_gu, 2, axis=-1)
    return (jax.nn.silu(g) * u) @ w_down

def partial_rope(t, pos):
    half = ROT_DIM // 2
    inv_freq = ROPE_THETA ** (-2.0 * jnp.arange(half, dtype=jnp.float32) / ROT_DIM)
    ang = pos.astype(jnp.float32)[:, None] * inv_freq[None, :]
    cos, sin = jnp.cos(ang), jnp.sin(ang)
    t1, t2 = t[..., :half], t[..., half:ROT_DIM]
    return jnp.concatenate([t1 * cos - t2 * sin, t2 * cos + t1 * sin, t[..., ROT_DIM:]], axis=-1)

def mlstm_scan(q, k, v, log_i, log_f):
    B, H, S, Dk = q.shape
    Dv = v.shape[-1]
    lc = min(M_CHUNK, S)
    nc = S // lc

    def chunks(t):
        return jnp.moveaxis(t.reshape((B, H, nc, lc) + t.shape[3:]), 2, 0)

    xs = (chunks(q), chunks(k), chunks(v), chunks(log_i), chunks(log_f))
    tril = jnp.tril(jnp.ones((lc, lc), dtype=bool))

    def step(carry, inp):
        C, n, m = carry
        q_c, k_c, v_c, li, lf = inp
        b = jnp.cumsum(lf, axis=-1)
        a_inter = b + m[..., None]
        d = jnp.where(tril, b[..., :, None] - b[..., None, :] + li[..., None, :], NEG_INF)
        m_t = jnp.maximum(a_inter, jnp.max(d, axis=-1))
        w_inter = jnp.exp(a_inter - m_t)
        s = jnp.exp(d - m_t[..., None]) * jnp.einsum('bhtd,bhsd->bhts', q_c, k_c)
        num = (w_inter[..., None] * jnp.einsum('bhvd,bhtd->bhtv', C, q_c)
               + jnp.einsum('bhts,bhsv->bhtv', s, v_c))
        den = w_inter * jnp.einsum('bhd,bhtd->bht', n, q_c) + jnp.sum(s, axis=-1)
        h = num / jnp.maximum(jnp.abs(den), jnp.exp(-m_t))[..., None]
        b_end = b[..., -1]
        g = b_end[..., None] - b + li
        m_new = jnp.maximum(b_end + m, jnp.max(g, axis=-1))
        decay = jnp.exp(b_end + m - m_new)
        wg = jnp.exp(g - m_new[..., None])
        C_new = decay[..., None, None] * C + jnp.einsum('bhs,bhsv,bhsd->bhvd', wg, v_c, k_c)
        n_new = decay[..., None] * n + jnp.einsum('bhs,bhsd->bhd', wg, k_c)
        return (C_new, n_new, m_new), h

    init = (jnp.zeros((B, H, Dv, Dk), jnp.float32), jnp.zeros((B, H, Dk), jnp.float32),
            jnp.full((B, H), NEG_INF, jnp.float32))
    _, hs = lax.scan(step, init, xs)
    return jnp.moveaxis(hs, 0, 2).reshape(B, H, S, Dv)

def bidirectional_mlstm(q, k, v, li_f, lf_f, li_b, lf_b):
    h_fwd = mlstm_scan(q, k, v, li_f, lf_f)
    flip = lambda t: jnp.flip(t, axis=2)
    h_bwd = flip(mlstm_scan(flip(q), flip(k), flip(v), flip(li_b), flip(lf_b)))
    return h_fwd + h_bwd

def dilated_band_attention(q, k, v, dilation, n_side):
    B, H, S, Dh = q.shape
    L = S // dilation

    def to_sub(t):
        return t.reshape(B, H, L, dilation, Dh).transpose(0, 1, 3, 2, 4)

    blk = n_side
    nb = -(-L // blk)
    lp = nb * blk
    qs = jnp.pad(to_sub(q), ((0, 0),) * 3 + ((0, lp - L), (0, 0)))
    kpad = ((0, 0),) * 3 + ((n_side, lp - L + n_side), (0, 0))
    ks = jnp.pad(to_sub(k), kpad)
    vs = jnp.pad(to_sub(v), kpad)
    qb = qs.reshape(B, H, dilation, nb, blk, Dh)

    def windows(t):
        tb = t.reshape(B, H, dilation, nb + 2, blk, Dh)
        return jnp.concatenate([tb[:, :, :, :-2], tb[:, :, :, 1:-1], tb[:, :, :, 2:]], axis=4)

    kw, vw = windows(ks), windows(vs)
    s = jnp.einsum('bhrnqe,bhrnke->bhrnqk', qb, kw)
    qi = jnp.arange(blk)[:, None]
    kk = jnp.arange(3 * blk)[None, :]
    band = jnp.abs(kk - n_side - qi) <= n_side
    key_idx = jnp.arange(nb)[:, None] * blk + kk - n_side
    in_range = (key_idx >= 0) & (key_idx < L)
    mask = band[None, :, :] & in_range[:, None, :]
    s = jnp.where(mask, s, NEG_INF)
    m = jnp.max(s, axis=-1, keepdims=True)
    p = jnp.exp(s - m)
    den = jnp.sum(p, axis=-1)
    o = jnp.einsum('bhrnqk,bhrnke->bhrnqe', p, vw) / den[..., None]
    lse = m[..., 0] + jnp.log(den)
    o = o.reshape(B, H, dilation, lp, Dh)[:, :, :, :L].transpose(0, 1, 3, 2, 4).reshape(B, H, S, Dh)
    lse = lse.reshape(B, H, dilation, lp)[..., :L].transpose(0, 1, 3, 2).reshape(B, H, S)
    return o, lse

def dilated_attention(q, k, v):
    outs, lses = [], []
    for w, d in zip(WINDOWS, DILATIONS):
        o, l = dilated_band_attention(q, k, v, d, w // (2 * d))
        outs.append(o)
        lses.append(l)
    wts = jax.nn.softmax(jnp.stack(lses), axis=0)
    return jnp.sum(wts[..., None] * jnp.stack(outs), axis=0)

def hybrid_mixer(h, w_in, gate_bias, g_q, g_k, g_mh, w_out):
    B, S, _ = h.shape
    proj = (h @ w_in).astype(jnp.float32)
    idx, acc = [], 0
    for n_cols in IN_SPLITS[:-1]:
        acc += n_cols
        idx.append(acc)
    mq, mk, mv, mo, mg, aq, ak, av = jnp.split(proj, idx, axis=-1)

    def heads(t, n):
        return t.reshape(B, S, n, -1).transpose(0, 2, 1, 3)

    gates = mg.reshape(B, S, 4, M_HEADS).transpose(2, 0, 3, 1) + gate_bias.astype(jnp.float32)[:, None, :, None]
    hm = bidirectional_mlstm(heads(mq, M_HEADS), heads(mk, M_HEADS) * (M_QK_DIM ** -0.5), heads(mv, M_HEADS),
                             gates[0], jax.nn.log_sigmoid(gates[1]), gates[2], jax.nn.log_sigmoid(gates[3]))
    hm = rms_norm(hm.transpose(0, 2, 1, 3), g_mh.reshape(M_HEADS, M_V_DIM))
    hm = (hm * jax.nn.sigmoid(mo.reshape(B, S, M_HEADS, M_V_DIM))).reshape(B, S, M_HEADS * M_V_DIM)

    pos = jnp.arange(S)
    qa = partial_rope(rms_norm(heads(aq, A_HEADS), g_q), pos) * (A_HEAD_DIM ** -0.5)
    ka = partial_rope(rms_norm(heads(ak, A_HEADS), g_k), pos)
    ha = dilated_attention(qa, ka, heads(av, A_HEADS))
    ha = ha.transpose(0, 2, 1, 3).reshape(B, S, A_HEADS * A_HEAD_DIM)

    return jnp.concatenate([hm, ha], axis=-1).astype(h.dtype) @ w_out

def first_inputs(seed: int = 0) -> dict:
    key = jax.random.key(seed)
    ks = jax.random.split(key, 20)
    f32 = jnp.float32

    def nrm(k, shape, scale):
        return jax.random.normal(k, shape, f32) * scale

    gate_bias = (nrm(ks[9], (DEPTH, 4, M_HEADS), 0.1)
                 + jnp.array([0.0, 1.0, 0.0, 1.0], f32)[None, :, None]
                 * jnp.linspace(3.0, 6.0, M_HEADS, dtype=f32)[None, None, :])
    return {
        'x': nrm(ks[0], (BATCH, SEQ, D_MODEL), 1.0),
        'c': nrm(ks[1], (BATCH, D_MODEL), 1.0),
        'w_ada': nrm(ks[2], (DEPTH, D_MODEL, N_MOD * D_MODEL), 0.5 * D_MODEL ** -0.5),
        'b_ada': nrm(ks[3], (DEPTH, N_MOD * D_MODEL), 0.02),
        'g_ffn1': 1.0 + nrm(ks[4], (DEPTH, D_MODEL), 0.02),
        'w_gu1': nrm(ks[5], (DEPTH, D_MODEL, 2 * D_FF), D_MODEL ** -0.5),
        'w_down1': nrm(ks[6], (DEPTH, D_FF, D_MODEL), D_FF ** -0.5),
        'g_mix': 1.0 + nrm(ks[7], (DEPTH, D_MODEL), 0.02),
        'w_in': nrm(ks[8], (DEPTH, D_MODEL, IN_COLS), D_MODEL ** -0.5),
        'gate_bias': gate_bias,
        'g_q': 1.0 + nrm(ks[10], (DEPTH, A_HEAD_DIM), 0.02),
        'g_k': 1.0 + nrm(ks[11], (DEPTH, A_HEAD_DIM), 0.02),
        'g_mh': 1.0 + nrm(ks[12], (DEPTH, M_HEADS * M_V_DIM), 0.02),
        'w_out': nrm(ks[13], (DEPTH, MIX_WIDTH, D_MODEL), MIX_WIDTH ** -0.5),
        'g_ffn2': 1.0 + nrm(ks[14], (DEPTH, D_MODEL), 0.02),
        'w_gu2': nrm(ks[15], (DEPTH, D_MODEL, 2 * D_FF), D_MODEL ** -0.5),
        'w_down2': nrm(ks[16], (DEPTH, D_FF, D_MODEL), D_FF ** -0.5),
        'g_final': 1.0 + nrm(ks[17], (DEPTH, D_MODEL), 0.02),
    }

def first_block(x, c, w_ada, b_ada, g_ffn1, w_gu1, w_down1, g_mix, w_in, gate_bias, g_q, g_k, g_mh,
              w_out, g_ffn2, w_gu2, w_down2, g_final):
    B, S, D = x.shape
    cs = jax.nn.silu(c)
    for l in range(DEPTH):
        mod = (cs @ w_ada[l] + b_ada[l]).reshape(B, N_MOD, D)[:, :, None, :]
        sh1, sc1, gt1, sh2, sc2, gt2, sh3, sc3, gt3 = [mod[:, i] for i in range(N_MOD)]
        h = modulate(rms_norm(x, g_ffn1[l]), sh1, sc1)
        x = x + HALF_STEP * gt1 * swiglu(h, w_gu1[l], w_down1[l])
        h = modulate(rms_norm(x, g_mix[l]), sh2, sc2)
        x = x + gt2 * hybrid_mixer(h, w_in[l], gate_bias[l], g_q[l], g_k[l], g_mh[l], w_out[l])
        h = modulate(rms_norm(x, g_ffn2[l]), sh3, sc3)
        x = x + HALF_STEP * gt3 * swiglu(h, w_gu2[l], w_down2[l])
        x = rms_norm(x, g_final[l])
    return x


DEPTH_2 = 2

RMS_EPS = 1e-6
LN_EPS = 1e-5
MIX_WIDTH_2 = D_MODEL
POOL_WIDTH = MIX_WIDTH_2 // 2
POOL_WINDOWS = (2, 4, 8, 16)
POOL_GROUPS = len(POOL_WINDOWS)
POOL_GROUP_DIM = POOL_WIDTH // POOL_GROUPS
SSM_WIDTH = MIX_WIDTH_2 - POOL_WIDTH
SSM_GROUP_DIM = 16
SSM_GROUPS = SSM_WIDTH // SSM_GROUP_DIM
SSM_STATE = 64
DT_MIN = 0.001
DT_MAX = 0.1
CONV_CHANNELS = D_MODEL
CONV_KERNEL = 31
N_EVEN = (DEPTH_2 + 1) // 2
N_ODD = DEPTH_2 // 2


def _rmsnorm(x, g):
    x32 = x.astype(jnp.float32)
    y = x32 * lax.rsqrt(jnp.mean(x32 * x32, axis=-1, keepdims=True) + RMS_EPS)
    return (y * g.astype(jnp.float32)).astype(x.dtype)

def _multiscale_pool(u, pool_w, pool_scale):
    b, s, _ = u.shape
    u32 = u.astype(jnp.float32).reshape(b, s, POOL_GROUPS, POOL_GROUP_DIM)
    csum = jnp.cumsum(u32, axis=1)
    pos = jnp.arange(1, s + 1, dtype=jnp.float32)[None, :, None]
    outs = []
    for g, w in enumerate(POOL_WINDOWS):
        c = csum[:, :, g, :]
        lag = jnp.pad(c, ((0, 0), (w, 0), (0, 0)))[:, :s, :]
        outs.append((c - lag) / jnp.minimum(pos, float(w)) - u32[:, :, g, :])
    pooled = jnp.stack(outs, axis=2)
    mixed = jnp.einsum('bsgc,gcd->bsgd', pooled, pool_w.astype(jnp.float32))
    return (mixed.reshape(b, s, POOL_WIDTH) * pool_scale.astype(jnp.float32)).astype(u.dtype)

def _scan_combine(left, right):
    a1r, a1i, b1r, b1i = left
    a2r, a2i, b2r, b2i = right
    ar = a2r * a1r - a2i * a1i
    ai = a2r * a1i + a2i * a1r
    br = a2r * b1r - a2i * b1i + b2r
    bi = a2r * b1i + a2i * b1r + b2i
    return (ar, ai, br, bi)

def _s5(u, log_dt, a_re, a_im, b_re, b_im, c_re, c_im, d_skip, w_glu):
    bsz, s, _ = u.shape
    f32 = jnp.float32
    u32 = u.astype(f32).reshape(bsz, s, SSM_GROUPS, SSM_GROUP_DIM)
    dt = jnp.exp(log_dt.astype(f32))[:, None]
    ar = a_re.astype(f32)
    ai = a_im.astype(f32)
    mag = jnp.exp(ar * dt)
    ang = ai * dt
    abar_re = mag * jnp.cos(ang)
    abar_im = mag * jnp.sin(ang)
    den = ar * ar + ai * ai
    nr = abar_re - 1.0
    ni = abar_im
    k_re = (nr * ar + ni * ai) / den
    k_im = (ni * ar - nr * ai) / den
    br = b_re.astype(f32)
    bi = b_im.astype(f32)
    bb_re = k_re[..., None] * br - k_im[..., None] * bi
    bb_im = k_re[..., None] * bi + k_im[..., None] * br
    bu_re = jnp.einsum('bsgh,gph->bsgp', u32, bb_re)
    bu_im = jnp.einsum('bsgh,gph->bsgp', u32, bb_im)
    shape = bu_re.shape
    _, _, x_re, x_im = lax.associative_scan(
        _scan_combine,
        (jnp.broadcast_to(abar_re, shape), jnp.broadcast_to(abar_im, shape), bu_re, bu_im),
        axis=1)
    y = (jnp.einsum('bsgp,ghp->bsgh', x_re, c_re.astype(f32))
         - jnp.einsum('bsgp,ghp->bsgh', x_im, c_im.astype(f32)))
    y = y.reshape(bsz, s, SSM_WIDTH) + d_skip.astype(f32) * u32.reshape(bsz, s, SSM_WIDTH)
    gv = jnp.einsum('bsc,ce->bse', y, w_glu.astype(f32))
    val, gate = jnp.split(gv, 2, axis=-1)
    return (val * jax.nn.sigmoid(gate)).astype(u.dtype)

def _even_mixer(h, w_in, pool_w, pool_scale, log_dt, a_re, a_im, b_re, b_im,
                c_re, c_im, d_skip, w_glu, w_out):
    proj = jnp.einsum('bsd,de->bse', h, w_in)
    u_pool = proj[..., :POOL_WIDTH]
    u_ssm = proj[..., POOL_WIDTH:MIX_WIDTH_2]
    z = proj[..., MIX_WIDTH_2:]
    y_pool = _multiscale_pool(u_pool, pool_w, pool_scale)
    y_ssm = _s5(u_ssm, log_dt, a_re, a_im, b_re, b_im, c_re, c_im, d_skip, w_glu)
    y = jnp.concatenate([y_pool, y_ssm], axis=-1) * jax.nn.silu(z)
    return jnp.einsum('bse,ed->bsd', y, w_out)

def _odd_mixer(h, w_in, conv_w, conv_b, ln_g, ln_b, w_out):
    proj = jnp.einsum('bsd,de->bse', h, w_in)
    val = proj[..., :CONV_CHANNELS]
    gt = proj[..., CONV_CHANNELS:2 * CONV_CHANNELS]
    z = proj[..., 2 * CONV_CHANNELS:]
    g = (val * jax.nn.sigmoid(gt)).astype(jnp.float32)
    kern = conv_w.astype(jnp.float32)[:, None, :]
    c = lax.conv_general_dilated(
        g, kern, window_strides=(1,), padding=[(CONV_KERNEL - 1, 0)],
        dimension_numbers=('NWC', 'WIO', 'NWC'), feature_group_count=CONV_CHANNELS)
    c = c + conv_b.astype(jnp.float32)
    mu = jnp.mean(c, axis=-1, keepdims=True)
    cc = c - mu
    var = jnp.mean(cc * cc, axis=-1, keepdims=True)
    c = cc * lax.rsqrt(var + LN_EPS) * ln_g.astype(jnp.float32) + ln_b.astype(jnp.float32)
    y = (jax.nn.silu(c) * jax.nn.silu(z.astype(jnp.float32))).astype(h.dtype)
    return jnp.einsum('bse,ed->bsd', y, w_out)

def second_inputs(seed: int = 0) -> dict:
    key = jax.random.key(seed)
    ks = jax.random.split(key, 24)
    f32 = jnp.float32

    def nrm(k, shape, scale):
        return jax.random.normal(k, shape, f32) * scale

    n_idx = jnp.arange(SSM_STATE, dtype=f32)
    a_im0 = jnp.broadcast_to(math.pi * n_idx, (N_EVEN, SSM_GROUPS, SSM_STATE))
    return {
        "x": jax.random.normal(ks[0], (BATCH, SEQ, D_MODEL), f32),
        "even_norm": 1.0 + nrm(ks[1], (N_EVEN, D_MODEL), 0.05),
        "even_w_in": nrm(ks[2], (N_EVEN, D_MODEL, 2 * MIX_WIDTH_2), D_MODEL ** -0.5),
        "pool_w": nrm(ks[3], (N_EVEN, POOL_GROUPS, POOL_GROUP_DIM, POOL_GROUP_DIM), POOL_GROUP_DIM ** -0.5),
        "pool_scale": 1.0 + nrm(ks[4], (N_EVEN, POOL_WIDTH), 0.05),
        "ssm_log_dt": jax.random.uniform(ks[5], (N_EVEN, SSM_GROUPS), f32,
                                         math.log(DT_MIN), math.log(DT_MAX)),
        "ssm_a_re": -0.5 * jnp.exp(nrm(ks[6], (N_EVEN, SSM_GROUPS, SSM_STATE), 0.05)),
        "ssm_a_im": a_im0 + nrm(ks[7], (N_EVEN, SSM_GROUPS, SSM_STATE), 0.01),
        "ssm_b_re": nrm(ks[8], (N_EVEN, SSM_GROUPS, SSM_STATE, SSM_GROUP_DIM), (2 * SSM_GROUP_DIM) ** -0.5),
        "ssm_b_im": nrm(ks[9], (N_EVEN, SSM_GROUPS, SSM_STATE, SSM_GROUP_DIM), (2 * SSM_GROUP_DIM) ** -0.5),
        "ssm_c_re": nrm(ks[10], (N_EVEN, SSM_GROUPS, SSM_GROUP_DIM, SSM_STATE), SSM_STATE ** -0.5),
        "ssm_c_im": nrm(ks[11], (N_EVEN, SSM_GROUPS, SSM_GROUP_DIM, SSM_STATE), SSM_STATE ** -0.5),
        "ssm_d": nrm(ks[12], (N_EVEN, SSM_WIDTH), 1.0),
        "ssm_w_glu": nrm(ks[13], (N_EVEN, SSM_WIDTH, 2 * SSM_WIDTH), SSM_WIDTH ** -0.5),
        "even_w_out": nrm(ks[14], (N_EVEN, MIX_WIDTH_2, D_MODEL), MIX_WIDTH_2 ** -0.5),
        "odd_norm": 1.0 + nrm(ks[15], (N_ODD, D_MODEL), 0.05),
        "odd_w_in": nrm(ks[16], (N_ODD, D_MODEL, 3 * CONV_CHANNELS), D_MODEL ** -0.5),
        "conv_w": nrm(ks[17], (N_ODD, CONV_KERNEL, CONV_CHANNELS), CONV_KERNEL ** -0.5),
        "conv_b": nrm(ks[18], (N_ODD, CONV_CHANNELS), 0.02),
        "conv_ln_g": 1.0 + nrm(ks[19], (N_ODD, CONV_CHANNELS), 0.05),
        "conv_ln_b": nrm(ks[20], (N_ODD, CONV_CHANNELS), 0.02),
        "odd_w_out": nrm(ks[21], (N_ODD, CONV_CHANNELS, D_MODEL), CONV_CHANNELS ** -0.5),
        "final_norm": 1.0 + nrm(ks[22], (D_MODEL,), 0.05),
    }

def second_block(x, even_norm, even_w_in, pool_w, pool_scale, ssm_log_dt, ssm_a_re, ssm_a_im,
              ssm_b_re, ssm_b_im, ssm_c_re, ssm_c_im, ssm_d, ssm_w_glu, even_w_out,
              odd_norm, odd_w_in, conv_w, conv_b, conv_ln_g, conv_ln_b, odd_w_out, final_norm):
    for i in range(DEPTH_2):
        j = i // 2
        if i % 2 == 0:
            h = _rmsnorm(x, even_norm[j])
            x = x + _even_mixer(h, even_w_in[j], pool_w[j], pool_scale[j], ssm_log_dt[j],
                                ssm_a_re[j], ssm_a_im[j], ssm_b_re[j], ssm_b_im[j],
                                ssm_c_re[j], ssm_c_im[j], ssm_d[j], ssm_w_glu[j], even_w_out[j])
        else:
            h = _rmsnorm(x, odd_norm[j])
            x = x + _odd_mixer(h, odd_w_in[j], conv_w[j], conv_b[j], conv_ln_g[j],
                               conv_ln_b[j], odd_w_out[j])
    return _rmsnorm(x, final_norm)


def setup_inputs(seed=0):
    out = dict(first_inputs(seed))
    for name, value in second_inputs(seed + 1).items():
        if name != "x":
            out[name + "_2"] = value
    return out


def reference(
    x, c, w_ada, b_ada, g_ffn1, w_gu1, w_down1, g_mix, w_in, gate_bias, g_q, g_k, g_mh, w_out,
    g_ffn2, w_gu2, w_down2, g_final, even_norm_2, even_w_in_2, pool_w_2, pool_scale_2,
    ssm_log_dt_2, ssm_a_re_2, ssm_a_im_2, ssm_b_re_2, ssm_b_im_2, ssm_c_re_2, ssm_c_im_2,
    ssm_d_2, ssm_w_glu_2, even_w_out_2, odd_norm_2, odd_w_in_2, conv_w_2, conv_b_2, conv_ln_g_2,
    conv_ln_b_2, odd_w_out_2, final_norm_2,
):
    x = first_block(
        x, c, w_ada, b_ada, g_ffn1, w_gu1, w_down1, g_mix, w_in, gate_bias, g_q, g_k, g_mh,
        w_out, g_ffn2, w_gu2, w_down2, g_final,
    )
    return second_block(
        x, even_norm_2, even_w_in_2, pool_w_2, pool_scale_2, ssm_log_dt_2, ssm_a_re_2,
        ssm_a_im_2, ssm_b_re_2, ssm_b_im_2, ssm_c_re_2, ssm_c_im_2, ssm_d_2, ssm_w_glu_2,
        even_w_out_2, odd_norm_2, odd_w_in_2, conv_w_2, conv_b_2, conv_ln_g_2, conv_ln_b_2,
        odd_w_out_2, final_norm_2,
    )


_drawn_inputs = setup_inputs


def setup_inputs(seed=0):
    import zlib

    import numpy as np

    out = dict(_drawn_inputs(seed))
    spreads = {}
    factors = {'g_ffn1': 8.0,
     'g_mix': 7.428,
     'g_q': 8.0,
     'g_k': 8.0,
     'g_mh': 64.0,
     'g_ffn2': 8.0,
     'pool_scale_2': 3.244,
     'ssm_log_dt_2': 19.77,
     'ssm_a_re_2': 64.0,
     'ssm_a_im_2': 19.319,
     'ssm_b_re_2': 30.32,
     'ssm_b_im_2': 29.632,
     'ssm_c_re_2': 30.032,
     'ssm_c_im_2': 30.176,
     'conv_b_2': 4.371,
     'conv_ln_g_2': 2.742,
     'conv_ln_b_2': 8.0}
    for name, (base, spread) in spreads.items():
        noise = np.random.default_rng([zlib.crc32(name.encode()), seed]).standard_normal(out[name].shape)
        drawn = base * np.exp(spread * noise) if base else spread * noise
        out[name] = __import__('jax').numpy.asarray(drawn.astype(out[name].dtype))
    for name, factor in factors.items():
        out[name] = (out[name] * factor).astype(out[name].dtype)
    return out
```

```python
from contextlib import ExitStack

import numpy as np

import concourse.bass as bass
from concourse import mybir

F32 = mybir.dt.float32
F32R = mybir.dt.float32r
ALU = mybir.AluOpType
ACT = mybir.ActivationFunctionType

P = 128
S = 512
D = 1024
KT = D // P
ST = S // P
FF = 2816
HALF = FF // P // 2
RING = 4
EPS = 1e-6

T_MIX = 6 * HALF
T_OUT = T_MIX + 25
T_FFN = [0, T_OUT + KT]
T_EVEN = T_FFN[1] + 6 * HALF
T_GLU = T_EVEN + 16
T_EOUT = T_GLU + 4
T_ODD = T_EOUT + KT
T_OOUT = T_ODD + 3 * KT
T_END = T_OOUT + KT
X_FFN = [0, 3 * KT]
X_MIX = 2 * KT
X_FIN, X_EVEN, X_ODD = 5 * KT, 6 * KT, 7 * KT
N_FIN, N_EVEN, N_ODD, N_LAST = 3, 4, 5, 6

SH, GP, LEVELS = 16, 16, 9
TWO_PI = 2 * np.pi
MAGIC = 1.5 * 2 ** 23
TURN = [6.28125, 0.0019350051879882812, 3.019916050561733e-07]
EVEN_IN = 16
EVEN_TILES = [4, 5, 6, 7, 8, 0, 9, 1, 10, 2, 11, 3, 12, 13, 14, 15]
MAT = 8
GLU_TILES = [0, 2, 1, 3]
TAPS = 31
POOL_TAPS = 12

MH, AH, DH = 4, 8, 64
IN_TILES = ([("gates", 0, 1536)] + [("mq", t, t * P) for t in range(2)] + [("mk", t, 256 + t * P) for t in range(2)]
            + [("aq", t, 1552 + t * P) for t in range(4)] + [("ak", t, 2064 + t * P) for t in range(4)]
            + [("mv", t, 512 + t * P) for t in range(4)] + [("av", t, 2576 + t * P) for t in range(4)]
            + [("mo", t, 1024 + t * P) for t in range(4)])
GR = 36

SPANS = [[(st, st * P, S) for st in range(ST)], [(st, 0, (st + 1) * P) for st in reversed(range(ST))]]

C_C, G_FFN1, G_MIX, G_FFN2, G_FINAL, G_EVEN, G_ODD, CONV_B, LN_G, LN_B, G_LAST = range(0, 88, 8)
G_MH, POOL_SC, D_SKIP, G_Q, G_K, GATE_B, N_COLS = 88, 92, 96, 100, 101, 102, 103
ROWS = [("c", C_C, 8), ("g_ffn1", G_FFN1, 8), ("g_mix", G_MIX, 8), ("g_ffn2", G_FFN2, 8),
        ("g_final", G_FINAL, 8), ("even_norm_2", G_EVEN, 8), ("odd_norm_2", G_ODD, 8),
        ("conv_b_2", CONV_B, 8), ("conv_ln_g_2", LN_G, 8), ("conv_ln_b_2", LN_B, 8),
        ("final_norm_2", G_LAST, 8), ("g_mh", G_MH, 4), ("pool_scale_2", POOL_SC, 4),
        ("ssm_d_2", D_SKIP, 4)]
ADA_ORDER = [1, 0]


def constants():
    f = np.float32
    t, s = np.meshgrid(np.arange(S), np.arange(S), indexing="ij")
    dist = np.abs(t - s)
    count = (dist <= 64) * 1 + (dist % 4 == 0) * (dist <= 256) + (dist % 16 == 0)
    ln_count = np.where(count > 0, np.log(np.maximum(count, 1)), -1e30).astype(f)
    u, v = np.meshgrid(np.arange(P), np.arange(P), indexing="ij")
    causal = np.stack([np.where(v >= u, 0, -1e30), np.where(v <= u, 0, -1e30)], 1).astype(f)
    half = DH // 8
    inv_freq = f(500000.0) ** (f(-2.0) * np.arange(half, dtype=f) / f(2 * half))
    ang = np.arange(S, dtype=f)[None, :] * inv_freq[:, None]
    cos, sin = np.ones((DH, S), f), np.zeros((DH, S), f)
    cos[:half] = cos[half:2 * half] = np.cos(ang)
    sin[:half], sin[half:2 * half] = -np.sin(ang), np.sin(ang)
    swap = np.zeros((P, P), f)
    for base in (0, DH):
        for r in range(half):
            swap[base + half + r, base + r] = swap[base + r, base + half + r] = 1
    heads = np.kron(np.eye(2, dtype=f), np.ones((DH, DH), f))
    strip = np.zeros((P, 2 * GR - 1), f)
    strip[:, GR - 1] = 1
    pick = np.zeros((16, 2 * GR), f)
    for h in range(MH):
        pick[h, h] = pick[8 + h, 32 + h] = 1
        pick[4 + h, GR + h] = pick[12 + h, GR + 32 + h] = 1
    edge = np.stack([w / np.minimum(np.arange(16) + 1.0, w) for w in (2, 4, 8, 16)]).astype(f)
    pairs = np.zeros((2, DH, 4, 8, SH), f)
    for q in range(4):
        for par in range(2):
            pairs[par, :, q, 2 * q + par] = 1
    return {"pairs": pairs.reshape(P, 4, P), "pool_edge": np.ascontiguousarray(np.broadcast_to(edge, (P, 4, 16))), "ident": np.eye(P, dtype=f), "ln_count": ln_count, "causal": causal,
            "rope_cos": np.tile(cos, (2, 1)), "rope_sin": np.tile(sin, (2, 1)),
            "swap": swap, "head_ones": heads, "strip": strip, "pick": pick}


def upto(eng, sem, value):
    if isinstance(value, int) and value <= 0:
        return
    eng.wait_ge(sem, value)


def rounds(eng, first, last, body, peel=False):
    if peel:
        body(first)
        first += 1
    if first < last:
        with eng.Fori(first, last) as i:
            body(i)


def rounds_aside(eng, last, body, aside):
    if aside is None:
        return rounds(eng, 0, last, body)
    aside(0)
    rounds(eng, 0, 2, body)
    aside(1)
    rounds(eng, 2, 4, body)
    aside(2)
    rounds(eng, 4, last, body)


def build_program(nc, a, out):
    ctx = ExitStack()
    with ctx:
        place = [(nc.sbuf_base + 31) // 32 * 32]

        at_of = {}

        def sb(name, shape, dt=F32):
            n = 4 * int(np.prod(shape[1:]))
            off = place[0]
            place[0] += (n + 31) // 32 * 32
            at_of[name] = off
            return nc.alloc_sbuf_tensor_at(name, shape, dt, offset=off)

        def sem(name):
            return ctx.enter_context(nc.semaphore(name))

        xT = sb("xT", [P, KT, S])
        h_hi = sb("h_hi", [P, KT, S], F32R)
        h_lo = sb("h_lo", [P, KT, S], F32R)
        a_hi = sb("a_hi", [P, HALF * S], F32R)
        a_lo = sb("a_lo", [P, HALF * S], F32R)
        w_hi = sb("w_hi", [P, RING, KT, P], F32R)
        w_lo = sb("w_lo", [P, RING, KT, P], F32R)
        w_in = sb("w_stage", [P, RING, KT, P])
        ident = sb("ident", [P, P])
        ones = sb("ones", [P, P])
        cols = sb("cols", [P, N_COLS])
        bada = sb("bada", [P, 72])
        mod = sb("mod", [P, 72])
        gs = sb("gs", [P, 3 * KT])
        gate = sb("gate", [P, 3 * KT])
        cs = sb("cs", [P, KT])
        eps = sb("eps", [P, 1])
        rs = sb("rs", [P, S])
        sq = sb("sq", [P, 2, S])
        tmp = sb("tmp", [P, 2, S])
        tmp2 = sb("tmp2", [P, 2, S])
        mx = sb("mx", [P, 4, 4 * AH])
        arena = place[0]

        def region(start, size):
            at = [start]

            def put(name, shape, dt=F32):
                off = at[0]
                at[0] += (4 * int(np.prod(shape[1:])) + 31) // 32 * 32
                assert at[0] <= start + size, (name, at[0] - start - size)
                return nc.alloc_sbuf_tensor_at(name, shape, dt, offset=off)
            return put

        H_AT = at_of["h_hi"]
        put = region(arena, nc.sbuf_usable_end - arena)
        mq = put("mq", [P, 2, S])
        mk = put("mk", [P, 2, S])
        aq = put("aq", [P, 4, S])
        ak = put("ak", [P, 4, S])
        vm = put("vm", [P, ST, S])
        va = put("va", [P, ST, S])
        mo = put("mo", [P, MH, S])
        swap = put("swap", [P, P])
        head_ones = put("head_ones", [P, P])
        gcol = put("gcol", [P, ST, GR])
        put = region(at_of["a_hi"] + KT * S * 4, 3 * S * 4)
        rope_cos = put("rope_cos", [P, S])
        rope_sin = put("rope_sin", [P, S])
        neg_m = put("neg_m", [GR, S])
        put = region(at_of["a_lo"] + KT * S * 4, 3 * S * 4)
        exp_m = put("exp_m", [GR, S])
        gval = put("gval", [GR, S])
        causal = put("causal", [P, 2, P])
        strip = put("strip", [P, 2 * GR - 1])
        pick = put("pick", [16, 2 * GR])
        g16 = va[0:16, 3]
        rs2 = va[:, 0:2]
        qn = va[:, 2:4]
        z_g = mo[0:GR, 0]
        li_g = mo[0:GR, 1]
        e_g = mo[0:GR, 2]
        lf_g = mo[0:GR, 3]
        f_g = vm[0:GR, 0]
        m_g = vm[0:GR, 1]
        fm_g = vm[0:GR, 2]
        put = region(H_AT, 2 * KT * S * 4)
        dg = put("dg", [P, 2, ST, P])
        p_m = put("p_m", [P, 2, S])
        num = put("num", [P, 2 * MH, S])
        e_m = put("e_m", [P, 2, S])
        rsh = put("rsh", [P, 2, S])
        rs_of = [rsh[:, 0], rsh[:, 1], e_m[:, 0], e_m[:, 1]]
        den_r = rs[0:GR]
        put = region(H_AT, 2 * KT * S * 4)
        ln_count = put("ln_count", [P, ST, S])
        s_a = put("s_a", [P, 2, S])
        e_a = put("e_a", [P, 2, S])
        pt_a = put("pt_a", [P, 2, ST, S])

        put = region(arena, nc.sbuf_usable_end - arena)
        s_rows = put("s_rows", [80, P])
        s_ldt = put("s_ldt", [80, 2])
        c_rows = put("c_rows", [P, 2, 4, 2, DH])
        b_in = put("b_in", [P, 2, GP, SH])
        acol = put("acol", [P, 80])
        ccol = put("ccol", [P, 2, 4, P])
        bas = put("bas", [P, 24, GP])
        wp = put("wp", [P, LEVELS, 2, GP])
        bb = put("bb", [P, 2, GP, SH])
        bt = put("bt", [P, 4, GP, SH])
        pairs = put("pairs", [P, 4, P])
        xm = put("xm", [P, 2, MAT, P])
        wt_s = put("wt_s", [P, 2, MAT, P])
        tab_s = put("tab_s", [P, 2, 2, S])
        tab_t = put("tab_t", [P, 2, 2, S // 2])
        ct_s = wt_s[:, 1]
        xm_of = [xm[:, 0], xm[:, 1],
                 c_rows[:].rearrange("p r t d q -> p (r t d q)").rearrange("p (m q) -> p m q", q=P),
                 ccol[:].rearrange("p r t q -> p (r t) q")]
        put = region(arena, nc.sbuf_usable_end - arena)
        us = put("us", [P, 4, S])
        zs = put("zs", [P, 4, S])
        mats = put("mats", [P, 2, 2 * MAT, P])
        tab = put("tab", [P, 2, 2, S])
        pool_w = put("pool_w", [P, 4, P])
        edge = put("edge", [P, 4, 16])
        prods2 = put("prods2", [P, 4, S])
        put = region(at_of["a_hi"] + 4 * S * 4, 7 * S * 4)
        prods0 = put("prods0", [P, 4, S])
        pads = put("pads", [P, 2, 16 + S])
        put = region(at_of["a_lo"] + 4 * S * 4, 7 * S * 4)
        prods1 = put("prods1", [P, 4, S])
        pv = put("pv", [P, 2, 16 + S])
        prods = [prods0, prods1, prods2]
        zc = tmp
        zp = [sq[:, 0], sq[:, 1], tmp2[:, 0], tmp2[:, 1]]
        mag_c = mx[:, 0, 0:GP]
        put = region(arena, nc.sbuf_usable_end - arena)
        cv = put("cv", [P, KT, S])
        zo = put("zo", [P, KT, S])
        gb = put("gb", [P, 2, TAPS - 1 + S])
        pacc = put("pacc", [P, 2, S])
        cw = put("cw", [P, KT, TAPS])
        acc2 = put("acc2", [P, S])
        tap_of = [tmp2[:, 0], tmp2[:, 1], sq[:, 0], sq[:, 1]]
        cw_rows = put("cw_rows", [TAPS, D])
        ln_eps = put("ln_eps", [P, 1])
        put = region(arena, nc.sbuf_usable_end - arena)
        o_rows = put("o_rows", [P, ST, D])
        mats_d = nc.dram_tensor("mats_d", [4, P, 2 * MAT, P], F32).ap()
        tab_d = nc.dram_tensor("tab_d", [P, 2, GP, S], F32).ap()

        x_rows = sb("x_rows", [P, ST, D])
        ada_w = sb("ada_w", [P, 4, D])
        ada_acc = sb("ada_acc", [P, D])
        rows = sb("rows", [P, P])
        rows2 = sb("rows2", [P, P])

        ps = [ctx.enter_context(nc.psum_tensor(f"ps{i}", [P, S], F32)) for i in range(8)]

        w_loaded = [sem(f"w_loaded{i}") for i in range(RING)]
        w_hi_ready = sem("w_hi_ready")
        w_split = sem("w_split")
        w_used = sem("w_used")
        const_in, x_in, zeroed = sem("const_in"), sem("x_in"), sem("zeroed")
        cols_t, cols_ready, bada_ready = sem("cols_t"), sem("cols_ready"), sem("bada_ready")
        x_t, x_ready, silu_c = sem("x_t"), sem("x_ready"), sem("silu_c")
        ada_in = [sem(f"ada_in{i}") for i in range(4)]
        ada_done, ada_sum, mod_ready = sem("ada_done"), sem("ada_sum"), sem("mod_ready")
        sq_ready, sq_used, ln_ready, rs_ready = sem("sq_ready"), sem("sq_used"), sem("ln_ready"), sem("rs_ready")
        gs_ready = sem("gs_ready")
        hn_ready, h_hi_ready, hf_ready, h_ready = sem("hn_ready"), sem("h_hi_ready"), sem("hf_ready"), sem("h_ready")
        silu_ready, prod_ready, a_hi_ready, a_ready = sem("silu_ready"), sem("prod_ready"), sem("a_hi_ready"), sem("a_ready")
        down_done, x_new = sem("down_done"), sem("x_new")
        dve_self = sem("dve_self")
        mix_const = sem("mix_const")
        proj_read = sem("proj_read")
        g16_ready = sem("g16_ready")
        picked, g_chain = sem("picked"), sem("g_chain")
        lsig_e, lsig_l, em_ready = sem("lsig_e"), sem("lsig_l"), sem("em_ready")
        g_t, gcol_ready = sem("g_t"), sem("gcol_ready")
        qk_sum, qk_ln, qk_rs = sem("qk_sum"), sem("qk_ln"), sem("qk_rs")
        qk_n, qk_rot, qk_done = sem("qk_n"), sem("qk_rot"), sem("qk_done")
        v_t, v_done = sem("v_t"), sem("v_done")
        mo_done = sem("mo_done")
        bm_ready, sc_ready, dg_ready, e_ready = sem("bm_ready"), sem("sc_ready"), sem("dg_ready"), sem("e_ready")
        p_ready, p_used, num_ready = sem("p_ready"), sem("p_used"), sem("num_ready")
        den_ready, br_ready, hm_ready, hsq_ready = sem("den_ready"), sem("br_ready"), sem("hm_ready"), sem("hsq_ready")
        hsum, hln, hrs, hy_ready, mix_hi, mix_ready = (sem("hsum"), sem("hln"), sem("hrs"), sem("hy_ready"),
                                                       sem("mix_hi"), sem("mix_ready"))
        lnc_in, s_ready, s_max, s_exp, p_norm = sem("lnc_in"), sem("s_ready"), sem("s_max"), sem("s_exp"), sem("p_norm")
        pt_t, pt_ready, pv_ready = sem("pt_t"), [sem("pt_ready0"), sem("pt_ready1")], sem("pv_ready")
        s5_in, s5_rows, s5_t, s5_cols = sem("s5_in"), sem("s5_rows"), sem("s5_t"), sem("s5_cols")
        dt_ready, turn_ready, trig_ready, kk_ready = sem("dt_ready"), sem("turn_ready"), sem("trig_ready"), sem("kk_ready")
        xm_ready, wb_t, wb_copied, wb_stored = sem("xm_ready"), sem("wb_t"), sem("wb_copied"), sem("wb_stored")
        ct_stored, tab_made, tab_stored, pool_self = sem("ct_stored"), sem("tab_made"), sem("tab_stored"), sem("pool_self")
        mats_in = [[sem("b_in0"), sem("b_in1")], [sem("c_in0"), sem("c_in1")]]
        tab_in = [sem("tab_in0"), sem("tab_in1")]
        pool_in, pads_zero = sem("pool_in"), sem("pads_zero")
        even_read, bu_ready, m_ready, mi_ready = sem("even_read"), sem("bu_ready"), sem("m_ready"), sem("mi_ready")
        scanned, d_ready, xr_ready, xi_ready = sem("scanned"), sem("d_ready"), sem("xr_ready"), sem("xi_ready")
        cy_done, y_ready, pw_self, win_ready = sem("cy_done"), sem("y_ready"), sem("pw_self"), sem("win_ready")
        pd_ready, pool_mixed, pp_ready = sem("pd_ready"), sem("pool_mixed"), sem("pp_ready")
        yh_ready, yl_ready, glu_t, glu_read, gp_ready = (sem("yh_ready"), sem("yl_ready"), sem("glu_t"),
                                                         sem("glu_read"), sem("gp_ready"))
        cw_in, cw_t, cw_ready, odd_zero = sem("cw_in"), sem("cw_t"), sem("cw_ready"), sem("odd_zero")
        tap_ready, g_ready, odd_read, pool_tap = sem("tap_ready"), sem("g_ready"), sem("odd_read"), sem("pool_tap")
        tap_prod = sem("tap_prod")
        cv_ready, tap_done, mean_sum, cc_ready = sem("cv_ready"), sem("tap_done"), sem("mean_sum"), sem("cc_ready")
        out_done = sem("out_done")
        cq_ready, var_sum, lv_ready, lr_ready = sem("cq_ready"), sem("var_sum"), sem("lv_ready"), sem("lr_ready")
        cn_ready, cs_ready, yo_ready, fin_ready = sem("cn_ready"), sem("cs_ready"), sem("yo_ready"), sem("fin_ready")
        out_t, out_copied, out_stored = sem("out_t"), [sem("out_copied0"), sem("out_copied1")], sem("out_stored")

        block = ctx.enter_context(nc.Block())

        def sublayer(sub):
            return gs[:, sub * KT:(sub + 1) * KT], mod[:, 3 * sub * KT:(3 * sub + 1) * KT]

        w_gu = [a["w_gu1"][0], a["w_gu2"][0]]
        w_dn = [a["w_down1"][0], a["w_down2"][0]]

        def cols_of(w, at, n=P):
            return w.rearrange("(k p) n -> p k n", p=P)[:, :, bass.ds(at, n)]

        def rows_of(w, f):
            return w[bass.ds(f * P, P), :].rearrange("p (n q) -> p n q", q=P)

        @block.sync
        def _(sp):
            sp.wait_ge(zeroed, 1)
            for name, at, n in ROWS:
                src = a[name]
                src = src.rearrange("a b -> (a b)") if len(src.shape) == 2 else src
                sp.dma_start(rows[at:at + n, :], src.rearrange("(r q) -> r q", q=P)).then_inc(const_in, 16)
            for name, at in (("g_q", G_Q), ("g_k", G_K)):
                for k in range(2):
                    sp.dma_start(rows[at:at + 1, 64 * k:64 * k + 64], a[name]).then_inc(const_in, 16)
            sp.dma_start(rows[GATE_B:GATE_B + 1, 0:16],
                         a["gate_bias"].rearrange("o g h -> o (g h)")).then_inc(const_in, 16)
            sp.dma_start(ident[:], a["ident"]).then_inc(const_in, 16)
            sp.dma_start(rows2[0:72], a["b_ada"][0].rearrange("(r q) -> r q", q=P)).then_inc(const_in, 16)
            sp.dma_start(x_rows[:], a["x"][0].rearrange("(t p) d -> p t d", p=P)).then_inc(x_in, 16)

            def load(i, c, src):
                upto(sp, w_split, i * RING + (c - RING + 1))
                sp.dma_start(w_in[:, c % RING], src).then_inc(w_loaded[c % RING], 16)

            def ffn(n):
                for half in range(2):
                    t0, f0 = T_FFN[n] + half * 3 * HALF, half * HALF
                    for j in range(2):
                        load(0, t0 + j, cols_of(w_gu[n], f0 * P + j * FF))

                    def pair_of_hidden(i):
                        for j in range(4):
                            load(i, t0 + 2 + j, cols_of(w_gu[n], i * (2 * P) + (f0 + 1 + j // 2) * P + j % 2 * FF))
                    rounds(sp, 0, HALF // 2, pair_of_hidden, peel=(t0 == 0))

                    def down(i):
                        for j in range(4):
                            load(i, t0 + 2 * HALF + j, rows_of(w_dn[n], i * 4 + (f0 + j)))
                    rounds(sp, 0, 2, down)
                    for j in range(8, HALF):
                        load(0, t0 + 2 * HALF + j, rows_of(w_dn[n], f0 + j))

            ffn(0)
            for n, (what, _, at) in enumerate(IN_TILES):
                if what == "gates":
                    sp.wait_ge(w_split, T_MIX - RING + 1)
                    sp.dma_start(w_in[:, T_MIX % RING, :, 0:16], cols_of(a["w_in"][0], at, 16)) \
                        .then_inc(w_loaded[T_MIX % RING], 16)
                else:
                    load(0, T_MIX + n, cols_of(a["w_in"][0], at))
            for n in range(KT):
                load(0, T_OUT + n, cols_of(a["w_out"][0], n * P))
            ffn(1)
            for n in range(EVEN_IN):
                load(0, T_EVEN + n, cols_of(a["even_w_in_2"][0], EVEN_TILES[n] * P))
            for q in range(4):
                sp.wait_ge(w_split, T_GLU + q - RING + 1)
                sp.dma_start(w_in[:, (T_GLU + q) % RING].rearrange("p (k m) q -> p k (m q)", m=2),
                             a["ssm_w_glu_2"][0].rearrange("(k p) n -> p k n", p=P)
                             [:, :, GLU_TILES[q] * 2 * P:(GLU_TILES[q] + 1) * 2 * P]).then_inc(w_loaded[(T_GLU + q) % RING], 16)
            for n in range(KT):
                load(0, T_EOUT + n, cols_of(a["even_w_out_2"][0], n * P))
            for n in range(3 * KT):
                load(0, T_ODD + n, cols_of(a["odd_w_in_2"][0], [D, 0, 2 * D][n % 3] + n // 3 * P))
            for n in range(KT):
                load(0, T_OOUT + n, rows_of(a["odd_w_out_2"][0], n))
            for st in range(ST):
                sp.wait_ge(out_copied[0], st + 1)
                sp.wait_ge(out_copied[1], st + 1)
                sp.dma_start(out[st * P:(st + 1) * P, :], o_rows[:, st]).then_inc(out_stored, 16)
            sp.wait_ge(out_stored, 16 * ST)

        @block.gpsimd
        def _(pool):
            pool.memset(rows[:], 0.0).then_inc(zeroed, 1)
            pool.memset(ones[:], 1.0).then_inc(zeroed, 1)
            pool.memset(eps[:], EPS).then_inc(zeroed, 1)

            def ada_load(q, j, kt):
                upto(pool, ada_done, q * KT + (kt - 3))
                pool.dma_start(ada_w[:, kt % 4], a["w_ada"][0][kt * P:(kt + 1) * P, bass.ds(j * D, D)]) \
                    .then_inc(ada_in[kt % 4], 16)

            for q in range(2):
                for kt in range(KT):
                    ada_load(q, ADA_ORDER[q], kt)
            with pool.Fori(2, 9) as j:
                for kt in range(KT):
                    ada_load(j, j, kt)
            pool.wait_ge(prod_ready, 2 * HALF)
            pool.wait_ge(ada_done, 9 * KT)
            for tile, name in ((swap, "swap"), (head_ones, "head_ones")):
                pool.dma_start(tile[:], a[name]).then_inc(mix_const, 16)
            pool.wait_ge(w_used, T_MIX)
            for tile, name in ((pick, "pick"), (strip, "strip"), (causal, "causal"), (rope_cos, "rope_cos"),
                               (rope_sin, "rope_sin")):
                pool.dma_start(tile[:], a[name]).then_inc(mix_const, 16)
            pool.wait_ge(p_used, 8 * MH)
            pool.wait_ge(e_ready, 8 * MH)
            pool.dma_start(ln_count[:], a["ln_count"].rearrange("(t p) s -> p t s", p=P)).then_inc(lnc_in, 16)

            def set_up():
                pool.wait_ge(mix_ready, KT)
                pool.memset(s_rows[:], 0.0).then_inc(s5_rows, 1)
                pool.wait_ge(s5_rows, 1)
                pool.dma_start(s_rows[0:16], a["ssm_a_re_2"][0].rearrange("(g r) p -> g (r p)", r=2)).then_inc(s5_in, 16)
                pool.dma_start(s_rows[32:48], a["ssm_a_im_2"][0].rearrange("(g r) p -> g (r p)", r=2)) \
                    .then_inc(s5_in, 16)
                pool.dma_start(s_ldt[64:80], a["ssm_log_dt_2"][0].rearrange("(g r) -> g r", r=2)).then_inc(s5_in, 16)
                for ri, name in enumerate(("re", "im")):
                    pool.dma_start(b_in[:, ri], a[f"ssm_b_{name}_2"][0].rearrange("(g r) p h -> (r p) g h", r=2)) \
                        .then_inc(s5_in, 16)
                    for d in range(2):
                        pool.dma_start(c_rows[:, ri, :, d],
                                       a[f"ssm_c_{name}_2"][0].rearrange("(t g) h p -> (g h) t p", t=4)) \
                            .then_inc(s5_in, 16)
                pool.dma_start(pairs[:], a["pairs"]).then_inc(s5_in, 16)
                pool.wait_ge(s5_in, 16 * 10)
                for r in range(2):
                    ins = pool.tensor_copy(s_rows[64:80, r * DH:(r + 1) * DH],
                                           s_ldt[64:80, r:r + 1].to_broadcast([16, DH]))
                ins.then_inc(s5_rows, 1)
                count = [0]

                def link(ins):
                    count[0] += 1
                    ins.then_inc(pool_self, 1)
                    pool.wait_ge(pool_self, count[0])

                for t in range(4):
                    pool.wait_ge(s5_cols, 3)
                    upto(pool, ct_stored, 16 * t)
                    for ri in range(2):
                        ins = pool.tensor_tensor(ct_s[:, ri * 4:ri * 4 + 4], pairs[:],
                                                 ccol[:, ri, t].unsqueeze(1).to_broadcast([P, 4, P]), ALU.mult)
                    link(ins)
                    pool.dma_start(mats_d[t][:, MAT:], ct_s).then_inc(ct_stored, 16)
                pool.wait_ge(kk_ready, 1)
                k_re, k_im = (bas[:, k].unsqueeze(2).to_broadcast([P, GP, SH]) for k in (15, 16))
                pool.tensor_tensor(bt[:, 0], k_re, b_in[:, 0], ALU.mult)
                pool.tensor_tensor(bt[:, 1], k_im, b_in[:, 1], ALU.mult)
                pool.tensor_tensor(bt[:, 2], k_re, b_in[:, 1], ALU.mult)
                link(pool.tensor_tensor(bt[:, 3], k_im, b_in[:, 0], ALU.mult))
                pool.tensor_tensor(bb[:, 0], bt[:, 0], bt[:, 1], ALU.subtract)
                link(pool.tensor_tensor(bb[:, 1], bt[:, 2], bt[:, 3], ALU.add))
                for t in range(4):
                    for ri in range(2):
                        for q in range(4):
                            ins = pool.tensor_tensor(
                                xm_of[t][:, ri * 4 + q].rearrange("p (g h) -> p g h", h=SH),
                                pairs[:, q].rearrange("p (g h) -> p g h", h=SH),
                                bb[:, ri, 4 * t + q].unsqueeze(1).to_broadcast([P, 8, SH]), ALU.mult)
                        ins.then_inc(xm_ready, 1)
                w_r, w_i, t0, t1, t2, t3 = (bas[:, k] for k in range(18, 24))
                for k in range(LEVELS):
                    if k == 0:
                        c_, s_ = bas[:, 9], bas[:, 8]
                    else:
                        pool.tensor_tensor(t0, wp[:, k - 1, 0], wp[:, k - 1, 0], ALU.mult)
                        pool.tensor_tensor(t1, wp[:, k - 1, 1], wp[:, k - 1, 1], ALU.mult)
                        link(pool.tensor_tensor(t2, wp[:, k - 1, 0], wp[:, k - 1, 1], ALU.mult))
                        pool.tensor_tensor(w_r, t0, t1, ALU.subtract)
                        link(pool.tensor_scalar(w_i, t2, 2.0, None, ALU.mult))
                        c_, s_ = w_r, w_i
                    pool.tensor_tensor(t0, c_, c_, ALU.mult)
                    link(pool.tensor_tensor(t1, s_, s_, ALU.mult))
                    link(pool.tensor_tensor(t3, t0, t1, ALU.add))
                    link(pool.tensor_scalar(t0, t3, -0.5, 1.5, ALU.mult, ALU.add))
                    pool.tensor_tensor(wp[:, k, 0], c_, t0, ALU.mult)
                    link(pool.tensor_tensor(wp[:, k, 1], s_, t0, ALU.mult))
                pool.memset(tab_s[:, 0, :, 0:1], 1.0)
                link(pool.memset(tab_s[:, 1, :, 0:1], 0.0))

                def tables(i):
                    for k in range(LEVELS):
                        n = 1 << k
                        c_, s_ = (wp[:, k, r, bass.ds(i * 2, 2)].unsqueeze(2).to_broadcast([P, 2, n]) for r in range(2))
                        re, im = (tab_s[:, r, :, 0:n] for r in range(2))
                        re2, im2 = (tab_s[:, r, :, n:2 * n] for r in range(2))
                        pool.tensor_tensor(re2, re, c_, ALU.mult)
                        pool.tensor_tensor(tab_t[:, 0, :, 0:n], im, s_, ALU.mult)
                        pool.tensor_tensor(im2, re, s_, ALU.mult)
                        pool.tensor_tensor(tab_t[:, 1, :, 0:n], im, c_, ALU.mult).then_inc(tab_made, 1)
                        pool.wait_ge(tab_made, i * (2 * LEVELS) + (2 * k + 1))
                        pool.tensor_tensor(re2, re2, tab_t[:, 0, :, 0:n], ALU.subtract)
                        pool.tensor_tensor(im2, im2, tab_t[:, 1, :, 0:n], ALU.add).then_inc(tab_made, 1)
                        pool.wait_ge(tab_made, i * (2 * LEVELS) + (2 * k + 2))
                    pool.dma_start(tab_d[:, :, bass.ds(i * 2, 2)], tab_s[:]).then_inc(tab_stored, 16)
                    pool.wait_ge(tab_stored, i * 16 + 16)
                rounds(pool, 0, GP // 2, tables)

            def even_mixer():
                pool.wait_ge(tab_stored, 16 * GP // 2)
                pool.wait_ge(ct_stored, 16 * 4)
                pool.wait_ge(wb_stored, 16 * 4)

                def load_mats(t, way):
                    at = slice(way * MAT, (way + 1) * MAT)
                    pool.dma_start(mats[:, t % 2, at], mats_d[t][:, at]).then_inc(mats_in[way][t % 2], 16)

                def load_table(u):
                    pool.dma_start(tab[:, u % 2], tab_d[:, :, u]).then_inc(tab_in[u % 2], 16)

                def add_inputs(u):
                    pool.wait_ge(m_ready, u + 1)
                    pr = prods[u % 3]
                    pool.tensor_tensor(pr[:, 0], pr[:, 0], pr[:, 1], ALU.add)
                    pool.tensor_tensor(pr[:, 2], pr[:, 2], pr[:, 3], ALU.subtract).then_inc(mi_ready, 1)

                def add_states(u):
                    pool.wait_ge(d_ready, u + 1)
                    pr = prods[u % 3]
                    pool.tensor_tensor(pr[:, 0], pr[:, 0], pr[:, 1], ALU.subtract).then_inc(xr_ready, 1)

                def windows(g):
                    pool.wait_ge(even_read, 6 + 2 * g)
                    upto(pool, pd_ready, g)
                    src = pv[:, g % 2]
                    for k in range(g + 1):
                        dst = pads[:, k % 2]
                        step = 1 << k
                        pool.tensor_tensor(dst[:, 16:], src[:, 16:], src[:, 16 - step:16 + S - step], ALU.add) \
                            .then_inc(pw_self, 1)
                        src = dst
                        pool.wait_ge(pw_self, g * (g + 1) // 2 + (k + 1))
                    pool.tensor_tensor(src[:, 16:32], src[:, 16:32], edge[:, g], ALU.mult).then_inc(win_ready, 1)

                load_mats(0, 0)
                load_table(0)
                load_table(1)
                load_mats(0, 1)
                pool.dma_start(pool_w[:], a["pool_w_2"][0].rearrange("g c d -> c g d")).then_inc(pool_in, 16)
                pool.dma_start(edge[:], a["pool_edge"]).then_inc(pool_in, 16)
                load_mats(1, 0)
                load_mats(1, 1)
                pool.wait_ge(w_used, T_EVEN)
                pool.memset(pads[:, :, 0:16], 0.0)
                pool.memset(pv[:, :, 0:16], 0.0).then_inc(pads_zero, 1)
                pool.wait_ge(pads_zero, 1)
                pool.wait_ge(pool_in, 32)
                for n in range(1, GP + 2):
                    if n <= GP:
                        add_inputs(n - 1)
                    if n >= 2:
                        if n < GP:
                            pool.wait_ge(d_ready, n - 1)
                            load_table(n)
                        add_states(n - 2)
                    if n in (5, 7, 9, 11):
                        windows((n - 5) // 2)
                    if n in (5, 9):
                        pool.wait_ge(bu_ready, n - 1)
                        load_mats((n + 3) // 4, 0)
                    if n in (9, 13):
                        pool.wait_ge(cy_done, n - 5)
                        load_mats((n - 1) // 4, 1)

            def odd_mixer():
                pool.wait_ge(mix_ready, 2 * KT)
                pool.dma_start(cw_rows[:], a["conv_w_2"][0]).then_inc(cw_in, 16)
                pool.memset(ln_eps[:], 1e-5)
                pool.memset(gb[:, :, 0:TAPS - 1], 0.0).then_inc(odd_zero, 1)
                for t in range(KT):
                    pool.wait_ge(tap_ready, t + 1)
                    for m in range(t * POOL_TAPS, (t + 1) * POOL_TAPS):
                        upto(pool, pool_tap, m)
                        pool.wait_ge(tap_prod, m + 1)
                        pool.tensor_tensor(pacc[:, t % 2], pacc[:, t % 2], tap_of[m % 4], ALU.add).then_inc(pool_tap, 1)

            set_up()
            even_mixer()
            odd_mixer()

        @block.scalar
        def _(act):
            act.wait_ge(cols_ready, 1)
            act.activation(cs[:], cols[:, C_C:C_C + KT], ACT.Silu).then_inc(silu_c, 1)

            def hi(i, c):
                act.wait_ge(w_loaded[c % RING], i * 16 + (c // RING + 1) * 16)
                upto(act, w_used, i * RING + (c - RING + 1))
                act.activation(w_hi[:, c % RING], w_in[:, c % RING], ACT.Copy).then_inc(w_hi_ready, 1)

            def square(n, kt):
                upto(act, sq_used, n * KT + kt - 1)
                act.activation(sq[:, kt % 2], xT[:, kt], ACT.Square).then_inc(sq_ready, 1)

            def norm_rs(n):
                act.wait_ge(sq_used, (n + 1) * KT)
                act.activation(rs[:], ps[0][:], ACT.Ln, bias=eps[:], scale=1.0 / D).then_inc(ln_ready, 1)
                act.wait_ge(ln_ready, n + 1)
                act.activation(rs[:], rs[:], ACT.Exp, scale=-0.5).then_inc(rs_ready, 1)

            def modulate(n, m, scale, shift):
                for kt in range(KT):
                    i = m * KT + kt
                    act.wait_ge(hn_ready, i + 1)
                    upto(act, h_ready, i - 1)
                    act.activation(tmp2[:, kt % 2], tmp[:, kt % 2], ACT.Identity, scale=scale[:, kt:kt + 1],
                                   bias=0.0 if shift is None else shift[:, kt:kt + 1]).then_inc(hf_ready, 1)
                    act.wait_ge(hf_ready, i + 1)
                    act.activation(h_hi[:, kt], tmp2[:, kt % 2], ACT.Copy).then_inc(h_hi_ready, 1)

            def ffn(n, norm_after, aside=None):
                for half in range(2):
                    t0, F0 = T_FFN[n] + half * 3 * HALF, (2 * n + half) * HALF

                    def hidden(i, f):
                        for j in range(2):
                            hi(i, t0 + 2 * f + 2 + j)
                        act.wait_ge(w_used, i * 4 + (t0 + 2 * f + 1))
                        act.activation(tmp[:, f % 2], ps[2 * (f % 2)][:], ACT.Silu).then_inc(silu_ready, 1)
                        act.wait_ge(prod_ready, i * 2 + (F0 + f + 1))
                        act.activation(a_hi[:, bass.ds(i * (2 * S) + f * S, S)], tmp2[:, f % 2], ACT.Copy) \
                            .then_inc(a_hi_ready, 1)
                    hidden(0, 0)
                    if aside is None:
                        rounds(act, 0, HALF // 2, lambda i: [hidden(i, 1), hidden(i, 2)], peel=(t0 == 0))
                    else:
                        rounds_aside(act, HALF // 2, lambda i: [hidden(i, 1), hidden(i, 2)],
                                     lambda at: aside(half, at))
                    t1 = t0 + 2 * HALF
                    rounds(act, 0, 2, lambda i: [hi(i, t1 + 2 + j) for j in range(4)])
                    hi(0, t1 + 10)
                    hi(0, t1 + 11)
                    if half == 1:
                        for kt in range(KT):
                            act.wait_ge(x_new, X_FFN[n] + KT + kt + 1)
                            square(norm_after, kt)
                    hi(0, t1 + 12)

            for c in range(2):
                hi(0, c)
            for kt in range(KT):
                act.wait_ge(x_ready, kt + 1)
                square(0, kt)
            norm_rs(0)
            act.wait_ge(mod_ready, 2)
            act.wait_ge(gs_ready, 1)
            modulate(0, 0, *sublayer(0))
            ffn(0, 1)

            def project_posts():
                qk = v = 0
                for n in range(len(IN_TILES) + 1):
                    if n < len(IN_TILES):
                        what, t, _ = IN_TILES[n]
                        bank = ps[n % 4]
                        hi(0, T_MIX + n + 2)
                        act.wait_ge(w_used, T_MIX + n + 1)
                        if what == "mq":
                            act.activation(mq[:, t], bank[:], ACT.Copy).then_inc(proj_read, 1)
                        elif what == "mk":
                            act.activation(mk[:, t], bank[:], ACT.Copy, scale=0.125).then_inc(proj_read, 1)
                        elif what in ("aq", "ak"):
                            upto(act, qk_n, qk - 1)
                            act.activation(tmp[:, qk % 2], bank[:], ACT.Copy)
                            act.activation(tmp2[:, qk % 2], bank[:], ACT.Square).then_inc(proj_read, 1)
                            qk += 1
                        elif what in ("mv", "av"):
                            upto(act, v_t, v - 1)
                            act.activation(sq[:, v % 2], bank[:], ACT.Copy).then_inc(proj_read, 1)
                            v += 1
                        elif what == "mo":
                            act.activation(mo[:, t], bank[:], ACT.Tanh, scale=0.5).then_inc(proj_read, 1)
                    if n == 2:
                        act.wait_ge(g_chain, 3)
                        act.activation(e_g, e_g, ACT.Exp).then_inc(lsig_e, 1)
                        act.wait_ge(lsig_e, 1)
                        act.activation(e_g, e_g, ACT.Ln, bias=ones[0:GR, 0:1]).then_inc(lsig_l, 1)
                    if n == 4:
                        act.wait_ge(g_chain, 11)
                        act.activation(exp_m[:], fm_g, ACT.Exp, scale=-1.0).then_inc(em_ready, 1)
                    if n >= 1 and IN_TILES[n - 1][0] in ("aq", "ak"):
                        m = qk - 1 if IN_TILES[min(n, len(IN_TILES) - 1)][0] not in ("aq", "ak") else qk - 2
                        act.wait_ge(qk_sum, m + 1)
                        act.activation(rs2[:, m % 2], ps[6][:], ACT.Ln, bias=eps[:], scale=1.0 / DH).then_inc(qk_ln, 1)
                        act.wait_ge(qk_ln, m + 1)
                        act.activation(rs2[:, m % 2], rs2[:, m % 2], ACT.Exp, scale=-0.5).then_inc(qk_rs, 1)

            def mlstm():
                j = 0
                for u in range(2 * MH):
                    r = u % 2 * 32 + u // 2
                    for st, lo_t, hi_t in SPANS[u % 2]:
                        if j == 0:
                            act.wait_ge(gcol_ready, 1)
                            act.wait_ge(h_ready, 2 * KT)
                            act.wait_ge(w_used, T_OUT)
                        act.wait_ge(dg_ready, u + 1)
                        upto(act, p_ready, j - 1)
                        a0, a1 = (st * P + P, S) if u % 2 == 0 else (0, st * P)
                        if a1 > a0:
                            act.activation(e_m[:, j % 2, a0:a1], ps[u % 2][:, a0:a1], ACT.Exp,
                                           bias=gcol[:, st, r:r + 1])
                        act.activation(e_m[:, j % 2, st * P:st * P + P], dg[:, u % 2, st], ACT.Exp).then_inc(e_ready, 1)
                        j += 1
                    if u:
                        act.wait_ge(p_used, 4 * u)
                        act.activation(num[:, u - 1], ps[5 + (u - 1) % 2][:], ACT.Copy).then_inc(num_ready, 1)
                act.wait_ge(p_used, 8 * MH)
                act.activation(num[:, 2 * MH - 1], ps[5 + 1][:], ACT.Copy).then_inc(num_ready, 1)
                for h in range(MH):
                    act.wait_ge(hm_ready, h + 1)
                    upto(act, hsum, h - 1)
                    act.activation(sq[:, h % 2], num[:, 2 * h], ACT.Square).then_inc(hsq_ready, 1)
                for h in range(MH):
                    act.wait_ge(hsum, h + 1)
                    act.activation(rs_of[h], ps[4 + h][:], ACT.Ln, bias=eps[:], scale=1.0 / P).then_inc(hln, 1)
                for h in range(MH):
                    act.wait_ge(hln, h + 1)
                    act.activation(rs_of[h], rs_of[h], ACT.Exp, scale=-0.5).then_inc(hrs, 1)
                for h in range(MH):
                    act.wait_ge(hy_ready, h + 1)
                    act.activation(a_hi[:, h * S:(h + 1) * S], tmp2[:, h % 2], ACT.Copy).then_inc(mix_hi, 1)

            def attention():
                act.wait_ge(mix_ready, MH)
                for s in range(4 * AH + 2):
                    if s < 4 * AH:
                        act.wait_ge(s_max, s + 1)
                        upto(act, pt_t, s - 1)
                        act.activation(e_a[:, s % 2], s_a[:, s % 2], ACT.Exp, bias=mx[:, 1, s:s + 1],
                                       accum_out=mx[:, 2, s:s + 1]).then_inc(s_exp, 1)
                    if s >= 2 and s % 2 == 0:
                        copy_pt(act, s - 2)
                    if s >= 3 and (s - 3) % 8 == 7:
                        pair_hi((s - 3) // 8)
                pair_hi(3)

            def pair_hi(i):
                act.wait_ge(pv_ready, 2 * i + 2)
                act.activation(a_hi[:, (MH + i) * S:(MH + i + 1) * S], ps[6 + i % 2][:], ACT.Copy).then_inc(mix_hi, 1)

            def copy_pt(eng, s):
                head = s // 4
                eng.wait_ge(pt_t, s + 1)
                upto(eng, pv_ready, head - 1)
                eng.activation(pt_a[:, head % 2, :, (s % 4) * P:(s % 4 + 1) * P],
                               ps[3 + s % 3][:].rearrange("p (t q) -> p t q", q=P), ACT.Copy).then_inc(pt_ready[0], 1)

            def project_out(t0, x_before, norm_after):
                for n in range(KT):
                    if t0 + n + 2 < T_END:
                        hi(0, t0 + n + 2)
                    act.wait_ge(x_new, x_before + n + 1)
                    square(norm_after, n)

            norm_rs(1)
            act.wait_ge(gs_ready, 3)
            modulate(1, 1, *sublayer(1))
            project_posts()
            mlstm()
            attention()
            project_out(T_OUT, X_MIX, 2)

            def set_up(half, at):
                if (half, at) == (0, 0):
                    act.wait_ge(s5_cols, 1)
                    act.activation(bas[:, 0], acol[:, 64:80], ACT.Exp).then_inc(dt_ready, 1)
                if (half, at) == (0, 1):
                    act.wait_ge(turn_ready, 1)
                    act.activation(mag_c, bas[:, 1], ACT.Exp).then_inc(trig_ready, 1)
                    act.activation(bas[:, 8], bas[:, 4], ACT.Sin)
                    act.activation(bas[:, 9], bas[:, 6], ACT.Sin).then_inc(trig_ready, 1)
                if half == 1 and at in (1, 2):
                    act.wait_ge(wb_copied, 4 * at)
                    for t in (2 * at - 2, 2 * at - 1):
                        act.dma_start(mats_d[t][:, 0:MAT], wt_s[:, t % 2]).then_inc(wb_stored, 16)

            def even_mixer():
                for n in range(GP + 4):
                    if n < EVEN_IN:
                        hi(0, T_EVEN + n + 2)
                        act.wait_ge(w_used, T_EVEN + n + 1)
                        bank = ps[n % 2][:]
                        if n < 4:
                            if n == 0:
                                act.wait_ge(mats_in[0][0], 16)
                                act.wait_ge(h_ready, 4 * KT)
                            act.activation(us[:, n], bank, ACT.Copy).then_inc(even_read, 1)
                        elif n < 12 and n % 2 == 0:
                            act.activation(zp[(n - 4) // 2], bank, ACT.Silu).then_inc(even_read, 1)
                        elif n < 12:
                            g = (n - 5) // 2
                            act.wait_ge(pads_zero, 1)
                            upto(act, pool_mixed, g - 1)
                            act.activation(pv[:, g % 2, 16:], bank, ACT.Copy).then_inc(even_read, 1)
                        else:
                            act.activation(zs[:, n - 12], bank, ACT.Silu).then_inc(even_read, 1)
                    if n in (10, 12, 14, 16):
                        g = (n - 10) // 2
                        act.wait_ge(pp_ready, g + 1)
                        act.activation(a_hi[:, g * S:(g + 1) * S], zp[g], ACT.Copy).then_inc(mix_hi, 1)
                    if n in (17, 18, 19):
                        y_hi(n - 17)
                y_hi(3)
                for q in range(4):
                    hi(0, T_GLU + q + 2)
                    act.wait_ge(w_used, T_GLU + q // 2 * 2 + 2)
                    upto(act, glu_read, q - 1)
                    act.activation(tmp[:, q % 2], ps[[6, 7, 2, 3][q]][:], ACT.Tanh, scale=0.5).then_inc(glu_t, 1)
                    act.wait_ge(gp_ready, q + 1)
                    act.activation(a_hi[:, (4 + q) * S:(5 + q) * S], tmp2[:, q % 2], ACT.Copy).then_inc(mix_hi, 1)

            def y_hi(t):
                act.wait_ge(w_used, T_GLU)
                act.wait_ge(y_ready, t + 1)
                act.activation(h_hi[:, t], us[:, t], ACT.Copy).then_inc(yh_ready, 1)

            def odd_mixer():
                for n in range(3 * KT):
                    hi(0, T_ODD + n + 2)
                    act.wait_ge(w_used, T_ODD + n + 1)
                    t = n // 3
                    if n == 0:
                        act.wait_ge(h_ready, 5 * KT)
                    if n % 3 == 0:
                        upto(act, g_ready, t - 1)
                        act.activation(tmp[:, t % 2], ps[n % 4][:], ACT.Tanh, scale=0.5).then_inc(odd_read, 1)
                    if n % 3 == 2:
                        act.activation(zo[:, t], ps[n % 4][:], ACT.Silu).then_inc(odd_read, 1)
                        first_taps(t)
                    for k in range(*[(4, 8), (8, POOL_TAPS), (0, 4)][n % 3]):
                        if n >= 2:
                            tap(n // 3 - (n % 3 < 2), k)
                for k in range(4, POOL_TAPS):
                    tap(KT - 1, k)
                act.wait_ge(pool_tap, KT * POOL_TAPS)
                for t in range(KT):
                    act.wait_ge(cc_ready, t + 1)
                    upto(act, var_sum, t - 1)
                    act.activation(sq[:, t % 2], cv[:, t], ACT.Square).then_inc(cq_ready, 1)
                act.wait_ge(var_sum, KT)
                act.activation(rs[:], ps[7][:], ACT.Ln, bias=ln_eps[:], scale=1.0 / D).then_inc(lv_ready, 1)
                act.wait_ge(lv_ready, 1)
                act.activation(rs[:], rs[:], ACT.Exp, scale=-0.5).then_inc(lr_ready, 1)
                for t in range(KT + 1):
                    if t < 2:
                        hi(0, T_OOUT + 2 + t)
                    if t >= 3 and T_OOUT + t + 1 < T_END:
                        hi(0, T_OOUT + t + 1)
                    if t < KT:
                        act.wait_ge(cn_ready, t + 1)
                        upto(act, yo_ready, t - 1)
                        act.activation(tmp[:, t % 2], cv[:, t], ACT.Silu, scale=cols[:, LN_G + t:LN_G + t + 1],
                                       bias=cols[:, LN_B + t:LN_B + t + 1]).then_inc(cs_ready, 1)
                    if t >= 1:
                        act.wait_ge(yo_ready, t)
                        act.activation(a_hi[:, (t - 1) * S:t * S], zo[:, t - 1], ACT.Copy).then_inc(mix_hi, 1)

            def tap(t, k):
                m = t * POOL_TAPS + k
                upto(act, pool_tap, m - 3)
                act.activation(tap_of[m % 4], gb[:, t % 2, 2 + k:2 + k + S], ACT.Copy, scale=cw[:, t, 2 + k:3 + k]) \
                    .then_inc(tap_prod, 1)

            def first_taps(t):
                act.wait_ge(g_ready, t + 1)
                upto(act, cv_ready, t - 1)
                act.activation(cv[:, t], gb[:, t % 2, 0:S], ACT.Copy, scale=cw[:, t, 0:1])
                act.activation(pacc[:, t % 2], gb[:, t % 2, 1:1 + S], ACT.Identity, scale=cw[:, t, 1:2],
                               bias=cols[:, CONV_B + t:CONV_B + t + 1]).then_inc(tap_ready, 1)

            norm_rs(2)
            modulate(2, 2, *sublayer(2))
            ffn(1, N_FIN, set_up)
            norm_rs(N_FIN)
            for kt in range(KT):
                act.wait_ge(x_new, X_FIN + kt + 1)
                square(N_EVEN, kt)
            norm_rs(N_EVEN)
            modulate(N_EVEN, 3, cols[:, G_EVEN:G_EVEN + KT], None)
            even_mixer()
            project_out(T_EOUT, X_EVEN, N_ODD)
            norm_rs(N_ODD)
            modulate(N_ODD, 4, cols[:, G_ODD:G_ODD + KT], None)
            odd_mixer()
            for kt in range(KT):
                act.wait_ge(x_new, X_ODD + kt + 1)
                square(N_LAST, kt)
            norm_rs(N_LAST)
            for st in range(ST):
                act.wait_ge(out_t, KT)
                act.activation(o_rows[:, st, 0:S], ps[2 * st][:], ACT.Copy).then_inc(out_copied[0], 1)

        @block.vector
        def _(dve):
            chain = [0]

            def link(ins):
                chain[0] += 1
                ins.then_inc(dve_self, 1)
                dve.wait_ge(dve_self, chain[0])

            dve.wait_ge(cols_t, 1)
            dve.tensor_copy(cols[:], ps[0][:, 0:N_COLS]).then_inc(cols_ready, 1)
            dve.wait_ge(cols_t, 2)
            dve.tensor_copy(bada[:], ps[1][:, 0:72]).then_inc(bada_ready, 1)
            for i in range(KT):
                dve.wait_ge(x_t, i + 1)
                dve.tensor_copy(xT[:, i], ps[i][:]).then_inc(x_ready, 1)

            def lo(i, c):
                dve.wait_ge(w_hi_ready, i * RING + (c + 1))
                dve.tensor_tensor(w_lo[:, c % RING], w_in[:, c % RING], w_hi[:, c % RING].bitcast(F32),
                                  ALU.subtract).then_inc(w_split, 1)

            def ada_add(q, kt):
                dve.wait_ge(ada_in[kt % 4], q * 32 + (kt // 4 + 1) * 16)
                if kt == 0:
                    upto(dve, ada_sum, q)
                    dve.tensor_scalar(ada_acc[:], ada_w[:, 0], cs[:, 0:1], None, ALU.mult).then_inc(ada_done, 1)
                else:
                    dve.wait_ge(ada_done, q * KT + kt)
                    dve.scalar_tensor_tensor(ada_acc[:], ada_w[:, kt % 4], cs[:, kt:kt + 1], ada_acc[:],
                                             ALU.mult, ALU.add).then_inc(ada_done, 1)

            def ada_col(q, j):
                dve.wait_ge(ada_sum, q + 1)
                dve.tensor_tensor(mod[:, bass.ds(j * KT, KT)], ps[7][:, 0:KT], bada[:, bass.ds(j * KT, KT)],
                                  ALU.add).then_inc(mod_ready, 1)

            def scale_cols(sub, g):
                at = (3 * sub + 1) * KT
                dve.scalar_tensor_tensor(gs[:, sub * KT:(sub + 1) * KT], mod[:, at:at + KT], 1.0,
                                         cols[:, g:g + KT], ALU.add, ALU.mult).then_inc(gs_ready, 1)

            def modulate(n, m):
                dve.wait_ge(rs_ready, n + 1)
                for kt in range(KT + 1):
                    i = m * KT + kt
                    if kt < KT:
                        upto(dve, hf_ready, i - 1)
                        dve.tensor_tensor(tmp[:, kt % 2], xT[:, kt], rs[:], ALU.mult).then_inc(hn_ready, 1)
                    if kt:
                        dve.wait_ge(h_hi_ready, i)
                        dve.tensor_tensor(h_lo[:, kt - 1], tmp2[:, (kt - 1) % 2], h_hi[:, kt - 1].bitcast(F32),
                                          ALU.subtract).then_inc(h_ready, 1)

            def ffn(n, sub, ada, aside=None):
                for half in range(2):
                    t0, F0 = T_FFN[n] + half * 3 * HALF, (2 * n + half) * HALF

                    def hidden(i, f, q=None):
                        for j in range(2):
                            lo(i, t0 + 2 * f + 2 + j)
                            if q is not None:
                                for k in range(2):
                                    ada_add(q, 4 * (f - 1) + 2 * j + k)
                        dve.wait_ge(silu_ready, i * 2 + (F0 + f + 1))
                        dve.wait_ge(w_used, i * 4 + (t0 + 2 * f + 2))
                        dve.tensor_tensor(tmp2[:, f % 2], tmp[:, f % 2], ps[2 * (f % 2) + 1][:], ALU.mult) \
                            .then_inc(prod_ready, 1)
                        dve.wait_ge(a_hi_ready, i * 2 + (F0 + f + 1))
                        at = bass.ds(i * (2 * S) + f * S, S)
                        dve.tensor_tensor(a_lo[:, at], tmp2[:, f % 2], a_hi[:, at].bitcast(F32), ALU.subtract) \
                            .then_inc(a_ready, 1)

                    def two(i, q):
                        hidden(i, 1, q)
                        hidden(i, 2, q)
                        if q is not None:
                            ada_col(q, q)
                    hidden(0, 0)
                    with_ada = [HALF // 2, 2][half] if ada else 0
                    rounds(dve, 0, with_ada, lambda i: two(i, i + [2, 7][half]), peel=(t0 == 0))
                    if aside is None:
                        rounds(dve, with_ada, HALF // 2, lambda i: two(i, None))
                    else:
                        rounds_aside(dve, HALF // 2, lambda i: two(i, None), lambda at: aside(half, at))
                    t1 = t0 + 2 * HALF
                    if ada and half == 0:
                        dve.wait_ge(mod_ready, 3)
                        link(dve.tensor_scalar(gate[:, 0:KT], mod[:, 2 * KT:3 * KT], 0.5, None, ALU.mult))
                    if ada and half == 1:
                        dve.wait_ge(mod_ready, 9)
                        scale_cols(1, G_MIX)
                        scale_cols(2, G_FFN2)
                        link(dve.tensor_copy(gate[:, KT:2 * KT], mod[:, 5 * KT:6 * KT]))
                        link(dve.tensor_scalar(gate[:, 2 * KT:3 * KT], mod[:, 8 * KT:9 * KT], 0.5, None, ALU.mult))
                    rounds(dve, 0, 2, lambda i: [lo(i, t1 + 2 + j) for j in range(4)])
                    lo(0, t1 + 10)
                    lo(0, t1 + 11)
                    for kt in range(KT):
                        if kt < KT - 1:
                            dve.wait_ge(down_done, (2 * n + half) * (KT - 1) + kt + 1)
                        else:
                            dve.wait_ge(w_used, t1 + HALF)
                        if half:
                            dve.wait_ge(x_new, X_FFN[n] + kt + 1)
                        dve.scalar_tensor_tensor(xT[:, kt], ps[kt][:], gate[:, sub * KT + kt:sub * KT + kt + 1],
                                                 xT[:, kt], ALU.mult, ALU.add).then_inc(x_new, 1)
                    lo(0, t1 + 12)

            dve.wait_ge(silu_c, 1)
            for q in range(2):
                for kt in range(KT):
                    ada_add(q, kt)
                    if q == 1 and kt == 0:
                        ada_col(0, ADA_ORDER[0])
                if q == 0:
                    lo(0, 0)
                    lo(0, 1)
            ada_col(1, ADA_ORDER[1])
            dve.wait_ge(mod_ready, 2)
            scale_cols(0, G_FFN1)
            dve.wait_ge(gs_ready, 1)
            modulate(0, 0)
            ffn(0, 0, True)

            def project_posts():
                qk = v = g = 0
                for n in range(len(IN_TILES) + 2):
                    if n < len(IN_TILES):
                        what, t, _ = IN_TILES[n]
                        lo(0, T_MIX + n + 2)
                        if what == "gates":
                            dve.wait_ge(w_used, T_MIX + n + 1)
                            dve.wait_ge(ada_sum, 9)
                            dve.tensor_scalar(g16[:], ps[0][0:16, :], cols[0:16, GATE_B:GATE_B + 1], None,
                                              ALU.add).then_inc(g16_ready, 1)
                    if n >= 1 and n <= len(IN_TILES) and IN_TILES[n - 1][0] in ("mv", "av"):
                        dst = vm if v < 4 else va
                        dve.wait_ge(v_t, v + 1)
                        dve.tensor_copy(dst[:, :, (v % 4) * P:(v % 4 + 1) * P],
                                        ps[4 + v % 2][:].rearrange("p (t q) -> p t q", q=P)).then_inc(v_done, 1)
                        v += 1
                    if n >= 1 and n <= len(IN_TILES) and IN_TILES[n - 1][0] == "mo":
                        h = n - 1 - (len(IN_TILES) - MH)
                        dve.wait_ge(proj_read, n - 1)
                        dve.tensor_scalar(mo[:, h], mo[:, h], 0.5, 0.5, ALU.mult, ALU.add).then_inc(mo_done, 1)
                    if n == 1:
                        gates_1()
                    if n == 3:
                        gates_2()
                    if n == 6:
                        dve.wait_ge(g_t, 1)
                        dve.tensor_copy(gcol[:], ps[7][:, 0:ST * GR].rearrange("p (t r) -> p t r", r=GR)) \
                            .then_inc(gcol_ready, 1)
                    if 1 <= n <= len(IN_TILES) and IN_TILES[n - 1][0] in ("aq", "ak"):
                        m = qk
                        g_at = G_Q if m < 4 else G_K
                        dve.wait_ge(qk_rs, m + 1)
                        upto(dve, qk_rot, m - 1)
                        upto(dve, qk_done, m - 1)
                        dve.scalar_tensor_tensor(qn[:, m % 2], tmp[:, m % 2], cols[:, g_at:g_at + 1], rs2[:, m % 2],
                                                 ALU.mult, ALU.mult).then_inc(qk_n, 1)
                        qk += 1
                    if 2 <= n <= len(IN_TILES) + 1 and IN_TILES[n - 2][0] in ("aq", "ak"):
                        m = g
                        g += 1
                        dst = aq if m < 4 else ak
                        if m == 0:
                            dve.wait_ge(mix_const, 7 * 16)
                        dve.wait_ge(qk_n, m + 1)
                        link(dve.tensor_tensor(dst[:, m % 4], qn[:, m % 2], rope_cos[:], ALU.mult))
                        dve.wait_ge(qk_rot, m + 1)
                        link(dve.tensor_tensor(qn[:, m % 2], ps[7][:], rope_sin[:], ALU.mult))
                        dve.tensor_tensor(dst[:, m % 4], dst[:, m % 4], qn[:, m % 2], ALU.add).then_inc(qk_done, 1)

            def gates_1():
                dve.wait_ge(picked, 1)
                dve.tensor_copy(li_g, ps[6][0:GR, :]).then_inc(g_chain, 1)
                dve.tensor_copy(z_g, ps[7][0:GR, :]).then_inc(g_chain, 1)
                dve.wait_ge(g_chain, 2)
                dve.scalar_tensor_tensor(e_g, z_g, -1.0, z_g, ALU.mult, ALU.min).then_inc(g_chain, 1)

            def gates_2():
                dve.wait_ge(lsig_l, 1)
                dve.scalar_tensor_tensor(lf_g, z_g, 0.0, e_g, ALU.min, ALU.subtract).then_inc(g_chain, 1)
                dve.wait_ge(g_chain, 4)
                link(dve.memset(f_g, 0.0))
                link(dve.memset(m_g, 0.0))
                link(dve.memset(fm_g, 1.0))
                for rows_, step in (((0, 4), 1), ((32, 36), -1)):
                    r = slice(*rows_)
                    dve.tensor_tensor_scan(vm[r, 0, ::step], vm[r, 2, ::step], mo[r, 3, ::step], 0.0,
                                           ALU.mult, ALU.add).then_inc(g_chain, 1)
                dve.wait_ge(g_chain, 6)
                dve.tensor_tensor(gval[:], li_g, f_g, ALU.subtract).then_inc(g_chain, 1)
                dve.wait_ge(g_chain, 7)
                for rows_, step in (((0, 4), 1), ((32, 36), -1)):
                    r = slice(*rows_)
                    dve.tensor_tensor_scan(vm[r, 1, ::step], gval[r, ::step], gval[r, ::step], -1e30,
                                           ALU.max, ALU.max).then_inc(g_chain, 1)
                dve.wait_ge(g_chain, 9)
                dve.tensor_scalar(neg_m[:], m_g, -1.0, None, ALU.mult).then_inc(g_chain, 1)
                dve.tensor_tensor(fm_g, f_g, m_g, ALU.add).then_inc(g_chain, 1)

            def diagonals(u):
                r = u % 2 * 32 + u // 2
                dve.wait_ge(bm_ready, u + 1)
                if u == 0:
                    dve.wait_ge(h_ready, 2 * KT)
                    dve.wait_ge(w_used, T_OUT)
                upto(dve, e_ready, 4 * (u - 1))
                for st in range(ST):
                    ins = dve.scalar_tensor_tensor(dg[:, u % 2, st], ps[u % 2][:, st * P:(st + 1) * P],
                                                   gcol[:, st, r:r + 1], causal[:, u % 2], ALU.add, ALU.min)
                ins.then_inc(dg_ready, 1)

            def mlstm():
                j = 0
                diagonals(0)
                for u in range(2 * MH):
                    for st, lo_t, hi_t in SPANS[u % 2]:
                        dve.wait_ge(sc_ready, j + 1)
                        dve.wait_ge(e_ready, j + 1)
                        upto(dve, p_used, j - 1)
                        dve.tensor_tensor(p_m[:, j % 2, lo_t:hi_t], e_m[:, j % 2, lo_t:hi_t],
                                          ps[2 + j % 3][:, lo_t:hi_t], ALU.mult).then_inc(p_ready, 1)
                        j += 1
                        if j % 4 == 3 and u + 1 < 2 * MH:
                            diagonals(u + 1)
                dve.wait_ge(p_used, 8 * MH)
                dve.wait_ge(em_ready, 1)
                link(dve.tensor_scalar(den_r, ps[7][0:GR, :], -1.0, None, ALU.mult))
                link(dve.tensor_tensor(den_r, den_r, ps[7][0:GR, :], ALU.max))
                link(dve.tensor_tensor(den_r, den_r, exp_m[:], ALU.max))
                dve.reciprocal(den_r, den_r).then_inc(den_ready, 1)
                for h in range(MH):
                    dve.wait_ge(num_ready, 2 * h + 2)
                    dve.wait_ge(br_ready, 2 * h + 1)
                    dve.tensor_tensor(num[:, 2 * h], num[:, 2 * h], ps[2 * (h % 2)][:], ALU.mult)
                    dve.wait_ge(br_ready, 2 * h + 2)
                    link(dve.tensor_tensor(num[:, 2 * h + 1], num[:, 2 * h + 1], ps[2 * (h % 2) + 1][:], ALU.mult))
                    dve.tensor_tensor(num[:, 2 * h], num[:, 2 * h], num[:, 2 * h + 1], ALU.add).then_inc(hm_ready, 1)
                for h in range(MH + 1):
                    if h < MH:
                        dve.wait_ge(hm_ready, h + 1)
                        dve.wait_ge(hrs, h + 1)
                        dve.wait_ge(mo_done, h + 1)
                        upto(dve, mix_ready, h - 1)
                        upto(dve, mix_hi, h - 1)
                        link(dve.tensor_tensor(tmp[:, h % 2], num[:, 2 * h], rs_of[h], ALU.mult))
                        dve.scalar_tensor_tensor(tmp2[:, h % 2], tmp[:, h % 2], cols[:, G_MH + h:G_MH + h + 1],
                                                 mo[:, h], ALU.mult, ALU.mult).then_inc(hy_ready, 1)
                    if h:
                        dve.wait_ge(mix_hi, h)
                        dve.tensor_tensor(a_lo[:, (h - 1) * S:h * S], tmp2[:, (h - 1) % 2],
                                          a_hi[:, (h - 1) * S:h * S].bitcast(F32), ALU.subtract).then_inc(mix_ready, 1)

            def attention():
                dve.wait_ge(lnc_in, 16)
                for s in range(4 * AH + 2):
                    if s < 4 * AH:
                        dve.wait_ge(s_ready, s + 1)
                        upto(dve, s_exp, s - 1)
                        link(dve.tensor_tensor_reduce(s_a[:, s % 2], ps[s % 3][:], ln_count[:, s % 4], 1.0, -3e38,
                                                      ALU.add, ALU.max, mx[:, 0, s:s + 1]))
                        dve.tensor_scalar(mx[:, 1, s:s + 1], mx[:, 0, s:s + 1], -1.0, None, ALU.mult) \
                            .then_inc(s_max, 1)
                    if 1 <= s <= 4 * AH:
                        dve.wait_ge(s_exp, s)
                        link(dve.reciprocal(mx[:, 3, s - 1:s], mx[:, 2, s - 1:s]))
                        dve.tensor_scalar(e_a[:, (s - 1) % 2], e_a[:, (s - 1) % 2], mx[:, 3, s - 1:s], None, ALU.mult) \
                            .then_inc(p_norm, 1)
                    if s >= 2 and s % 2 == 1:
                        copy_pt(s - 2)
                    if s >= 3 and (s - 3) % 8 == 7:
                        pair_lo((s - 3) // 8)
                pair_lo(3)

            def pair_lo(i):
                dve.wait_ge(mix_hi, MH + i + 1)
                at = slice((MH + i) * S, (MH + i + 1) * S)
                dve.tensor_tensor(a_lo[:, at], ps[6 + i % 2][:], a_hi[:, at].bitcast(F32), ALU.subtract) \
                    .then_inc(mix_ready, 1)

            def copy_pt(s):
                head = s // 4
                dve.wait_ge(pt_t, s + 1)
                upto(dve, pv_ready, head - 1)
                dve.tensor_copy(pt_a[:, head % 2, :, (s % 4) * P:(s % 4 + 1) * P],
                                ps[3 + s % 3][:].rearrange("p (t q) -> p t q", q=P)).then_inc(pt_ready[1], 1)

            def project_out(t0, gates, bank0=1):
                for n in range(KT):
                    if t0 + n + 2 < T_END:
                        lo(0, t0 + n + 2)
                    dve.wait_ge(w_used, t0 + n + 1)
                    if gates is None:
                        dve.tensor_tensor(xT[:, n], ps[bank0 + n % 4][:], xT[:, n], ALU.add).then_inc(x_new, 1)
                    else:
                        dve.scalar_tensor_tensor(xT[:, n], ps[bank0 + n % 4][:], gates[:, n:n + 1], xT[:, n],
                                                 ALU.mult, ALU.add).then_inc(x_new, 1)

            link(dve.tensor_scalar(cols[:, G_Q:G_Q + 1], cols[:, G_Q:G_Q + 1], DH ** -0.5, None, ALU.mult))
            dve.wait_ge(gs_ready, 3)
            modulate(1, 1)
            project_posts()
            mlstm()
            attention()
            project_out(T_OUT, gate[:, KT:2 * KT])

            def set_up(half, at):
                b = lambda k: bas[:, k]
                ar, ai = acol[:, 0:GP], acol[:, 32:32 + GP]
                if (half, at) == (0, 0):
                    dve.wait_ge(s5_t, 1)
                    dve.tensor_copy(acol[:], ps[4][:, 0:80]).then_inc(s5_cols, 1)
                    dve.tensor_copy(ccol[:, 0].rearrange("p t q -> p (t q)"), ps[5][:]).then_inc(s5_cols, 1)
                    dve.tensor_scalar(ccol[:, 1].rearrange("p t q -> p (t q)"), ps[6][:], -1.0, None, ALU.mult) \
                        .then_inc(s5_cols, 1)
                if (half, at) == (0, 1):
                    dve.wait_ge(dt_ready, 1)
                    dve.tensor_tensor(b(1), ar, b(0), ALU.mult)
                    link(dve.tensor_tensor(b(2), ai, b(0), ALU.mult))
                    link(dve.tensor_scalar(b(3), b(2), 1 / TWO_PI, MAGIC, ALU.mult, ALU.add))
                    link(dve.tensor_scalar(b(3), b(3), MAGIC, None, ALU.subtract))
                    link(dve.scalar_tensor_tensor(b(4), b(3), -TURN[0], b(2), ALU.mult, ALU.add))
                    for part in TURN[1:]:
                        link(dve.scalar_tensor_tensor(b(4), b(3), -part, b(4), ALU.mult, ALU.add))
                    link(dve.tensor_scalar(b(4), b(4), 3.1415925, -3.1415925, ALU.min, ALU.max))
                    link(dve.scalar_tensor_tensor(b(5), b(4), -1.0, b(4), ALU.mult, ALU.max))
                    dve.tensor_scalar(b(6), b(5), -1.0, float(np.pi / 2), ALU.mult, ALU.add).then_inc(turn_ready, 1)
                if (half, at) == (0, 2):
                    dve.wait_ge(trig_ready, 2)
                    dve.tensor_tensor(b(10), mag_c, b(9), ALU.mult)
                    dve.tensor_tensor(b(11), mag_c, b(8), ALU.mult)
                    dve.tensor_tensor(b(13), ar, ar, ALU.mult)
                    link(dve.tensor_tensor(b(14), ai, ai, ALU.mult))
                    dve.tensor_scalar(b(12), b(10), 1.0, None, ALU.subtract)
                    link(dve.tensor_tensor(b(13), b(13), b(14), ALU.add))
                    dve.reciprocal(b(14), b(13))
                    dve.tensor_tensor(b(15), b(12), ar, ALU.mult)
                    dve.tensor_tensor(b(16), b(11), ar, ALU.mult)
                    dve.tensor_tensor(b(17), b(11), ai, ALU.mult)
                    link(dve.tensor_tensor(b(18), b(12), ai, ALU.mult))
                    dve.tensor_tensor(b(15), b(15), b(17), ALU.add)
                    link(dve.tensor_tensor(b(16), b(16), b(18), ALU.subtract))
                    dve.tensor_tensor(b(15), b(15), b(14), ALU.mult)
                    dve.tensor_tensor(b(16), b(16), b(14), ALU.mult).then_inc(kk_ready, 1)
                if half == 1 and at < 2:
                    for k in range(4):
                        dve.wait_ge(wb_t, 4 * at + k + 1)
                        if at or k >= 2:
                            dve.wait_ge(ct_stored, 16 * 4)
                        upto(dve, wb_stored, 32 * at)
                        dve.tensor_copy(wt_s[:, k // 2, k % 2 * 4:k % 2 * 4 + 4].rearrange("p q s -> p (q s)"),
                                        ps[4 + k][:]).then_inc(wb_copied, 1)

            def even_mixer():
                def turn(u):
                    pr, b0 = prods[u % 3], 4 + 2 * (u % 2)
                    dve.wait_ge(bu_ready, u + 1)
                    dve.wait_ge(tab_in[u % 2], 16 * (u // 2 + 1))
                    upto(dve, cy_done, u - 2)
                    if u == 0:
                        dve.wait_ge(w_used, T_EVEN + 1)
                    dve.tensor_tensor(pr[:, 0], tab[:, u % 2, 0], ps[b0][:], ALU.mult)
                    dve.tensor_tensor(pr[:, 1], tab[:, u % 2, 1], ps[b0 + 1][:], ALU.mult)
                    dve.tensor_tensor(pr[:, 2], tab[:, u % 2, 0], ps[b0 + 1][:], ALU.mult)
                    dve.tensor_tensor(pr[:, 3], tab[:, u % 2, 1], ps[b0][:], ALU.mult).then_inc(m_ready, 1)

                def states(u):
                    pr = prods[u % 3]
                    dve.wait_ge(mi_ready, u + 1)
                    upto(dve, d_ready, u)
                    for r in range(2):
                        dve.tensor_tensor_scan(zc[:, r], mag_c[:, u:u + 1].to_broadcast([P, S]), pr[:, 2 * r], 0.0,
                                               ALU.mult, ALU.add).then_inc(scanned, 1)
                    dve.wait_ge(scanned, 2 * u + 2)
                    dve.tensor_tensor(pr[:, 0], tab[:, u % 2, 0], zc[:, 0], ALU.mult)
                    dve.tensor_tensor(pr[:, 1], tab[:, u % 2, 1], zc[:, 1], ALU.mult)
                    dve.tensor_tensor(pr[:, 2], tab[:, u % 2, 1], zc[:, 0], ALU.mult)
                    dve.tensor_tensor(pr[:, 3], tab[:, u % 2, 0], zc[:, 1], ALU.mult).then_inc(d_ready, 1)
                    dve.wait_ge(d_ready, u + 1)
                    dve.tensor_tensor(pr[:, 2], pr[:, 2], pr[:, 3], ALU.add).then_inc(xi_ready, 1)

                def output(t):
                    dve.wait_ge(cy_done, 4 * t + 4)
                    dve.scalar_tensor_tensor(us[:, t], us[:, t], cols[:, D_SKIP + t:D_SKIP + t + 1], ps[3][:],
                                             ALU.mult, ALU.add).then_inc(y_ready, 1)

                def y_lo(t):
                    dve.wait_ge(yh_ready, t + 1)
                    dve.tensor_tensor(h_lo[:, t], us[:, t], h_hi[:, t].bitcast(F32), ALU.subtract).then_inc(yl_ready, 1)

                for n in range(GP + 4):
                    if n < EVEN_IN:
                        lo(0, T_EVEN + n + 2)
                    if n % 4 == 0 and n >= 8:
                        output(n // 4 - 2)
                    if 1 <= n <= GP:
                        turn(n - 1)
                    if 2 <= n <= GP + 1:
                        states(n - 2)
                    if n in (7, 9, 11, 13):
                        g = (n - 7) // 2
                        dve.wait_ge(win_ready, g + 1)
                        dve.scalar_tensor_tensor(pv[:, g % 2, 16:], pads[:, g % 2, 16:], 0.5 ** (g + 1),
                                                 pv[:, g % 2, 16:], ALU.mult, ALU.subtract).then_inc(pd_ready, 1)
                    if n in (9, 11, 13, 15):
                        g = (n - 9) // 2
                        dve.wait_ge(pool_mixed, g + 1)
                        dve.scalar_tensor_tensor(zp[g], ps[2][:], cols[:, POOL_SC + g:POOL_SC + g + 1], zp[g],
                                                 ALU.mult, ALU.mult).then_inc(pp_ready, 1)
                    if n in (11, 13, 15, 17):
                        g = (n - 11) // 2
                        dve.wait_ge(mix_hi, KT + g + 1)
                        at = slice(g * S, (g + 1) * S)
                        dve.tensor_tensor(a_lo[:, at], zp[g], a_hi[:, at].bitcast(F32), ALU.subtract) \
                            .then_inc(mix_ready, 1)
                    if n in (18, 19):
                        y_lo(n - 18)
                output(3)
                y_lo(2)
                y_lo(3)
                for q in range(4):
                    lo(0, T_GLU + q + 2)
                    dve.wait_ge(glu_t, q + 1)
                    dve.wait_ge(even_read, EVEN_IN)
                    upto(dve, mix_ready, KT + 4 + q - 1)
                    dve.scalar_tensor_tensor(tmp2[:, q % 2], tmp[:, q % 2], 1.0, ps[[4, 5, 0, 1][q]][:],
                                             ALU.add, ALU.mult).then_inc(glu_read, 1)
                    dve.wait_ge(glu_read, q + 1)
                    dve.scalar_tensor_tensor(tmp2[:, q % 2], tmp2[:, q % 2], 0.5, zs[:, q], ALU.mult, ALU.mult) \
                        .then_inc(gp_ready, 1)
                    dve.wait_ge(mix_hi, KT + 4 + q + 1)
                    at = slice((4 + q) * S, (5 + q) * S)
                    dve.tensor_tensor(a_lo[:, at], tmp2[:, q % 2], a_hi[:, at].bitcast(F32), ALU.subtract) \
                        .then_inc(mix_ready, 1)

            def odd_mixer():
                dve.wait_ge(cw_t, 1)
                dve.wait_ge(mix_ready, 2 * KT)
                dve.tensor_scalar(cw[:], ps[5][:, 0:KT * 32].rearrange("p (t k) -> p t k", k=32)[:, :, 0:TAPS],
                                  0.5, None, ALU.mult).then_inc(cw_ready, 1)
                dve.wait_ge(cw_ready, 1)
                dve.wait_ge(odd_zero, 1)
                first = 2 + POOL_TAPS
                left = TAPS - first

                def taps(t, begin, end):
                    dve.wait_ge(tap_ready, t + 1)
                    for k in range(begin, end):
                        acc = acc2[:] if (k - first) % 2 else cv[:, t]
                        upto(dve, tap_done, t * left + (k - first) - 1)
                        if k == first + 1:
                            upto(dve, cv_ready, t)
                            dve.tensor_scalar(acc, gb[:, t % 2, k:k + S], cw[:, t, k:k + 1], None, ALU.mult) \
                                .then_inc(tap_done, 1)
                        else:
                            dve.scalar_tensor_tensor(acc, gb[:, t % 2, k:k + S], cw[:, t, k:k + 1], acc,
                                                     ALU.mult, ALU.add).then_inc(tap_done, 1)

                def merge(t):
                    dve.wait_ge(tap_done, (t + 1) * left)
                    link(dve.tensor_tensor(cv[:, t], cv[:, t], acc2[:], ALU.add))
                    dve.wait_ge(pool_tap, (t + 1) * POOL_TAPS)
                    dve.tensor_tensor(cv[:, t], cv[:, t], pacc[:, t % 2], ALU.add).then_inc(cv_ready, 1)

                cut = [first, first + left // 3, first + 2 * left // 3, TAPS]
                for n in range(3 * KT + 3):
                    if n < 3 * KT:
                        lo(0, T_ODD + n + 2)
                    t = n // 3
                    if n % 3 == 0 and t >= 2:
                        merge(t - 2)
                    if n % 3 == 1 and n < 3 * KT:
                        dve.wait_ge(w_used, T_ODD + n + 1)
                        dve.wait_ge(odd_read, 2 * t + 1)
                        upto(dve, tap_done, (t - 1) * left)
                        upto(dve, tap_prod, (t - 1) * POOL_TAPS)
                        dve.scalar_tensor_tensor(gb[:, t % 2, TAPS - 1:], tmp[:, t % 2], 1.0, ps[n % 4][:],
                                                 ALU.add, ALU.mult).then_inc(g_ready, 1)
                    if t:
                        taps(t - 1, cut[n % 3], cut[n % 3 + 1])
                merge(KT - 1)
                dve.wait_ge(mean_sum, KT)
                for t in range(KT):
                    dve.scalar_tensor_tensor(cv[:, t], ps[6][:], -1.0 / D, cv[:, t], ALU.mult, ALU.add) \
                        .then_inc(cc_ready, 1)
                dve.wait_ge(lr_ready, 1)
                for t in range(KT + 2):
                    if t < 2:
                        lo(0, T_OOUT + 2 + t)
                    if t < KT:
                        dve.tensor_tensor(cv[:, t], cv[:, t], rs[:], ALU.mult).then_inc(cn_ready, 1)
                    if 1 <= t <= KT:
                        dve.wait_ge(cs_ready, t)
                        dve.tensor_tensor(zo[:, t - 1], tmp[:, (t - 1) % 2], zo[:, t - 1], ALU.mult).then_inc(yo_ready, 1)
                    if t >= 2:
                        dve.wait_ge(mix_hi, 2 * KT + t - 1)
                        at = slice((t - 2) * S, (t - 1) * S)
                        dve.tensor_tensor(a_lo[:, at], zo[:, t - 2], a_hi[:, at].bitcast(F32), ALU.subtract) \
                            .then_inc(mix_ready, 1)
                    if t >= 3 and T_OOUT + t + 1 < T_END:
                        lo(0, T_OOUT + t + 1)

            modulate(2, 2)
            ffn(1, 2, False, set_up)
            dve.wait_ge(rs_ready, N_FIN + 1)
            for kt in range(KT):
                dve.wait_ge(x_new, X_FIN)
                dve.scalar_tensor_tensor(xT[:, kt], xT[:, kt], cols[:, G_FINAL + kt:G_FINAL + kt + 1], rs[:],
                                         ALU.mult, ALU.mult).then_inc(x_new, 1)
            modulate(N_EVEN, 3)
            even_mixer()
            project_out(T_EOUT, None, 4)
            modulate(N_ODD, 4)
            odd_mixer()
            for n in range(KT):
                if n < KT - 1:
                    dve.wait_ge(out_done, n + 1)
                else:
                    dve.wait_ge(w_used, T_END)
                dve.tensor_tensor(xT[:, n], ps[n][:], xT[:, n], ALU.add).then_inc(x_new, 1)
            dve.wait_ge(rs_ready, N_LAST + 1)
            for kt in range(KT):
                dve.scalar_tensor_tensor(xT[:, kt], xT[:, kt], cols[:, G_LAST + kt:G_LAST + kt + 1], rs[:],
                                         ALU.mult, ALU.mult).then_inc(fin_ready, 1)
            for st in range(ST):
                dve.wait_ge(out_t, KT)
                dve.tensor_copy(o_rows[:, st, S:], ps[2 * st + 1][:]).then_inc(out_copied[1], 1)

        @block.tensor
        def _(pe):
            pe.wait_ge(const_in, 16 * (len(ROWS) + 4 + 1 + 2))
            pe.wait_ge(zeroed, 3)
            pe.transpose(ps[0][:, 0:N_COLS], rows[0:N_COLS, :], ident[0:N_COLS, 0:N_COLS]).then_inc(cols_t, 1)
            pe.transpose(ps[1][:, 0:72], rows2[0:72, :], ident[0:72, 0:72]).then_inc(cols_t, 1)
            pe.wait_ge(x_in, 16)
            pe.wait_ge(cols_ready, 1)
            pe.wait_ge(bada_ready, 1)
            for kt in range(KT):
                for st in range(ST):
                    mm = pe.transpose(ps[kt][:, st * P:(st + 1) * P], x_rows[:, st, kt * P:(kt + 1) * P], ident[:])
                mm.then_inc(x_t, 1)

            def norm_sum(n, kt):
                pe.wait_ge(sq_ready, n * KT + kt + 1)
                pe.matmul(ps[0][:], ones[:], sq[:, kt % 2], start=(kt == 0), stop=(kt == KT - 1)) \
                    .then_inc(sq_used, 1)

            def ada_reduce(q):
                pe.wait_ge(ada_done, q * KT + KT)
                upto(pe, mod_ready, q)
                for nt in range(KT):
                    mm = pe.matmul(ps[7][:, nt:nt + 1], ada_acc[:, nt * P:(nt + 1) * P], ones[:, 0:1],
                                   start=True, stop=True)
                mm.then_inc(ada_sum, 1)

            def three(bank, slot, k, rhs_hi, rhs_lo, start, stop):
                pe.matmul(bank, w_hi[:, slot, k], rhs_hi, start=start, stop=False, skip_group_check=True)
                pe.matmul(bank, w_hi[:, slot, k], rhs_lo, start=False, stop=False, skip_group_check=True)
                return pe.matmul(bank, w_lo[:, slot, k], rhs_hi, start=False, stop=stop, skip_group_check=True)

            def project(i, c, bank, h_from=None):
                pe.wait_ge(w_split, i * RING + (c + 1))
                for k in range(KT):
                    if h_from is not None:
                        pe.wait_ge(h_ready, h_from + k + 1)
                    mm = three(ps[bank][:], c % RING, k, h_hi[:, k], h_lo[:, k], k == 0, k == KT - 1)
                mm.then_inc(w_used, 1)

            def ffn(n, norm_before, norm_after, ada, aside=None):
                for half in range(2):
                    t0, F0 = T_FFN[n] + half * 3 * HALF, (2 * n + half) * HALF
                    before = X_FFN[n]

                    def hidden(i, f, h_from=None):
                        upto(pe, prod_ready, i * 2 + (F0 + f - 1))
                        for j in range(2):
                            project(i, t0 + 2 * f + j, 2 * (f % 2) + j, h_from if j == 0 else None)

                    def two(i, q):
                        hidden(i, 1)
                        hidden(i, 2)
                        if q is not None:
                            ada_reduce(q)
                    if half:
                        pe.wait_ge(x_new, before + 2)
                    hidden(0, 0, None if half else norm_before * KT)
                    if half:
                        pe.wait_ge(x_new, before + KT)
                    with_ada = [HALF // 2, 2][half] if ada else 0
                    rounds(pe, 0, with_ada, lambda i: two(i, i + [2, 7][half]), peel=(t0 == 0))
                    if aside is None:
                        rounds(pe, with_ada, HALF // 2, lambda i: two(i, None))
                    else:
                        rounds_aside(pe, HALF // 2, lambda i: two(i, None), lambda at: aside(half, at))
                        if half:
                            pe.wait_ge(wb_copied, 8)
                    t1 = t0 + 2 * HALF
                    pe.wait_ge(prod_ready, F0 + HALF)
                    if ada:
                        pe.wait_ge(mod_ready, [7, 9][half])
                    for j in range(8):
                        pe.wait_ge(w_split, t1 + j + 1)
                        pe.wait_ge(a_ready, F0 + j + 1)
                        for kt in range(KT):
                            mm = three(ps[kt][:], (t1 + j) % RING, kt, a_hi[:, j * S:(j + 1) * S],
                                       a_lo[:, j * S:(j + 1) * S], j == 0, False)
                        mm.then_inc(w_used, 1)
                    pe.wait_ge(w_split, t1 + HALF)
                    pe.wait_ge(a_ready, F0 + HALF)
                    for kt in range(KT):
                        for j in range(8, HALF):
                            mm = three(ps[kt][:], (t1 + j) % RING, kt, a_hi[:, j * S:(j + 1) * S],
                                       a_lo[:, j * S:(j + 1) * S], False, j == HALF - 1)
                            if kt == KT - 1:
                                mm.then_inc(w_used, 1)
                        if kt < KT - 1:
                            mm.then_inc(down_done, 1)
                        if half and kt >= 2:
                            norm_sum(norm_after, kt - 2)
                    if half:
                        norm_sum(norm_after, KT - 2)
                        norm_sum(norm_after, KT - 1)

            for kt in range(KT):
                if kt == 0:
                    pe.wait_ge(x_ready, 1)
                norm_sum(0, kt)
            pe.wait_ge(x_ready, KT)
            ada_reduce(0)
            ada_reduce(1)
            ffn(0, 0, 1, True)

            def project_in():
                qk = v = r = 0
                for n in range(len(IN_TILES) + 2):
                    if n < len(IN_TILES):
                        if n == 0:
                            pe.wait_ge(x_new, X_MIX)
                            pe.wait_ge(rs_ready, 2)
                        if n == 4:
                            pe.wait_ge(g16_ready, 1)
                        upto(pe, proj_read, n - 4)
                        project(0, T_MIX + n, n % 4, KT if n == 0 else None)
                    if n == 1:
                        pe.wait_ge(g16_ready, 1)
                        pe.wait_ge(mix_const, 7 * 16)
                        pe.matmul(ps[6][0:GR, :], pick[:, 0:GR], g16[:], start=True, stop=True)
                        pe.matmul(ps[7][0:GR, :], pick[:, GR:2 * GR], g16[:], start=True, stop=True).then_inc(picked, 1)
                    if n == 5:
                        pe.wait_ge(g_chain, 7)
                        for st in range(ST):
                            mm = pe.transpose(ps[7][:, st * GR:(st + 1) * GR], gval[:, st * P:(st + 1) * P],
                                              ident[0:GR, 0:GR])
                        mm.then_inc(g_t, 1)
                    if 1 <= n <= len(IN_TILES) and IN_TILES[n - 1][0] in ("mv", "av"):
                        pe.wait_ge(proj_read, n - 1)
                        upto(pe, v_done, v - 1)
                        for st in range(ST):
                            mm = pe.transpose(ps[4 + v % 2][:, st * P:(st + 1) * P], sq[:, v % 2, st * P:(st + 1) * P],
                                              ident[:])
                        mm.then_inc(v_t, 1)
                        v += 1
                    if 1 <= n <= len(IN_TILES) and IN_TILES[n - 1][0] in ("aq", "ak"):
                        pe.wait_ge(proj_read, n - 1)
                        if qk:
                            pe.wait_ge(qk_rs, qk)
                        pe.matmul(ps[6][:], head_ones[:], tmp2[:, qk % 2], start=True, stop=True).then_inc(qk_sum, 1)
                        qk += 1
                    if 2 <= n <= len(IN_TILES) + 1 and IN_TILES[n - 2][0] in ("aq", "ak"):
                        pe.wait_ge(qk_n, r + 1)
                        pe.wait_ge(gcol_ready, 1)
                        upto(pe, qk_done, r)
                        pe.matmul(ps[7][:], swap[:], qn[:, r % 2], start=True, stop=True).then_inc(qk_rot, 1)
                        r += 1

            def spread(bank, row, src):
                return pe.matmul(bank, ident[0:GR, row:row + 1].to_broadcast([GR, P]), src, start=True, stop=True)

            def mlstm():
                steps = [(u, st, a0, a1) for u in range(2 * MH) for st, a0, a1 in SPANS[u % 2]]

                def scores(j):
                    u, st, a0, a1 = steps[j]
                    h, off = u // 2, u // 2 % 2 * DH
                    if j % 4 == 0:
                        upto(pe, e_ready, 4 * (u - 1))
                        if u == 0:
                            pe.wait_ge(proj_read, len(IN_TILES) - 1)
                            pe.wait_ge(qk_done, 8)
                            pe.wait_ge(g_chain, 10)
                        spread(ps[u % 2][:], u % 2 * 32 + h, neg_m[:]).then_inc(bm_ready, 1)
                    upto(pe, p_ready, j - 2)
                    if j == 2:
                        pe.wait_ge(v_done, 8)
                    pe.matmul(ps[2 + j % 3][:, a0:a1], mk[off:off + DH, h // 2, st * P:(st + 1) * P],
                              mq[off:off + DH, h // 2, a0:a1], start=True, stop=True).then_inc(sc_ready, 1)

                def sums(j):
                    u, st, a0, a1 = steps[j]
                    h = u // 2
                    pe.wait_ge(p_ready, j + 1)
                    if j % 4 == 0:
                        upto(pe, num_ready, u - 1)
                    pe.matmul(ps[5 + u % 2][:, a0:a1], vm[:, st, h * P:(h + 1) * P], p_m[:, j % 2, a0:a1],
                              start=(j % 4 == 0), stop=(j % 4 == 3), skip_group_check=True)
                    row = u % 2 * 32 + h
                    pe.matmul(ps[7][0:GR, a0:a1], strip[:, GR - 1 - row:2 * GR - 1 - row], p_m[:, j % 2, a0:a1],
                              start=(j == 0), stop=(j == 8 * MH - 1), skip_group_check=True).then_inc(p_used, 1)

                scores(0)
                for j in range(8 * MH):
                    if j + 1 < 8 * MH:
                        scores(j + 1)
                    sums(j)
                pe.wait_ge(den_ready, 1)
                pe.wait_ge(num_ready, 2 * MH)
                for h in range(MH + 1):
                    if h < MH:
                        upto(pe, hm_ready, h - 1)
                        spread(ps[2 * (h % 2)][:], h, den_r).then_inc(br_ready, 1)
                        spread(ps[2 * (h % 2) + 1][:], 32 + h, den_r).then_inc(br_ready, 1)
                    if h:
                        pe.wait_ge(hsq_ready, h)
                        pe.matmul(ps[3 + h][:], ones[:], sq[:, (h - 1) % 2], start=True, stop=True).then_inc(hsum, 1)

            def attention():
                pe.wait_ge(mix_ready, MH)

                def back(s):
                    pe.wait_ge(p_norm, s + 1)
                    upto(pe, pt_ready[(s - 3) % 2], (s - 3) // 2 + 1)
                    for st in range(ST):
                        mm = pe.transpose(ps[3 + s % 3][:, st * P:(st + 1) * P], e_a[:, s % 2, st * P:(st + 1) * P],
                                          ident[:])
                    mm.then_inc(pt_t, 1)

                def values(a_):
                    off = a_ % 2 * DH
                    for k in range(2):
                        pe.wait_ge(pt_ready[k], 2 * a_ + 2)
                    if a_ >= 4 and a_ % 2 == 0:
                        pe.wait_ge(mix_ready, MH + a_ // 2 - 1)
                    for st in range(ST):
                        mm = pe.matmul(ps[6 + a_ // 2 % 2][off:off + DH, :], va[:, st, a_ * DH:(a_ + 1) * DH],
                                       pt_a[:, a_ % 2, st], start=(st == 0), stop=(st == ST - 1))
                    mm.then_inc(pv_ready, 1)

                for s in range(4 * AH + 3):
                    if s < 4 * AH:
                        head, tt = s // 4, s % 4
                        off = head % 2 * DH
                        upto(pe, s_max, s - 2)
                        pe.matmul(ps[s % 3][:], aq[off:off + DH, head // 2, tt * P:(tt + 1) * P],
                                  ak[off:off + DH, head // 2, :], start=True, stop=True).then_inc(s_ready, 1)
                    if 2 <= s < 4 * AH + 2:
                        back(s - 2)
                    if s >= 3 and (s - 3) % 4 == 3:
                        values((s - 3) // 4)

            def project_out(t0, mixed, x_before, norm_after, bank0=1):
                for n in range(KT):
                    c = t0 + n
                    pe.wait_ge(w_split, c + 1)
                    if n >= 4:
                        pe.wait_ge(x_new, x_before + n - 3)
                    for k in range(KT):
                        if n == 0:
                            pe.wait_ge(mix_ready, mixed + k + 1)
                        mm = three(ps[bank0 + n % 4][:], c % RING, k, a_hi[:, k * S:(k + 1) * S],
                                   a_lo[:, k * S:(k + 1) * S], k == 0, k == KT - 1)
                    mm.then_inc(w_used, 1)
                    if n >= 2:
                        norm_sum(norm_after, n - 2)
                norm_sum(norm_after, KT - 2)
                norm_sum(norm_after, KT - 1)

            def set_up(half, at):
                if (half, at) == (0, 0):
                    pe.wait_ge(s5_in, 16 * 10)
                    pe.wait_ge(s5_rows, 2)
                    pe.transpose(ps[4][:, 0:80], s_rows[:], ident[0:80, 0:80])
                    for ri in range(2):
                        for t in range(4):
                            mm = pe.transpose(ps[5 + ri][:, t * P:(t + 1) * P],
                                              c_rows[:, ri, t].rearrange("p d q -> p (d q)"), ident[:])
                    mm.then_inc(s5_t, 1)
                if (half, at) in ((1, 0), (1, 1)):
                    pe.wait_ge(xm_ready, 4 * (at + 1))
                    upto(pe, wb_copied, 4 * at)
                    for t in (2 * at, 2 * at + 1):
                        for ri in range(2):
                            for q in range(4):
                                mm = pe.transpose(ps[4 + 2 * (t % 2) + ri][:, q * P:(q + 1) * P],
                                                  xm_of[t][:, ri * 4 + q], ident[:])
                            mm.then_inc(wb_t, 1)

            def even_mixer():
                def inputs(u):
                    ct, q = u // 4, u % 4
                    pe.wait_ge(even_read, ct + 1)
                    pe.wait_ge(mats_in[0][ct % 2], 16 * (ct // 2 + 1))
                    upto(pe, m_ready, u - 1)
                    for ri in range(2):
                        mm = pe.matmul(ps[4 + 2 * (u % 2) + ri][:], mats[:, ct % 2, ri * 4 + q], us[:, ct],
                                       start=True, stop=True)
                    mm.then_inc(bu_ready, 1)

                def outputs(u):
                    ct, q = u // 4, u % 4
                    pe.wait_ge(xr_ready, u + 1)
                    pe.wait_ge(xi_ready, u + 1)
                    pe.wait_ge(mats_in[1][ct % 2], 16 * (ct // 2 + 1))
                    if q == 0:
                        upto(pe, y_ready, ct)
                    pe.matmul(ps[3][:], mats[:, ct % 2, MAT + q], prods[u % 3][:, 0], start=(q == 0), stop=False)
                    pe.matmul(ps[3][:], mats[:, ct % 2, MAT + 4 + q], prods[u % 3][:, 2], start=False,
                              stop=(q == 3)).then_inc(cy_done, 1)

                for n in range(GP + 4):
                    if 1 <= n <= GP:
                        inputs(n - 1)
                    if n < EVEN_IN:
                        if n == 0:
                            pe.wait_ge(rs_ready, N_EVEN + 1)
                        upto(pe, even_read, n - 1)
                        project(0, T_EVEN + n, n % 2, 3 * KT if n == 0 else None)
                    if n in (8, 10, 12, 14):
                        g = (n - 8) // 2
                        pe.wait_ge(pd_ready, g + 1)
                        upto(pe, pp_ready, g)
                        pe.matmul(ps[2][:], pool_w[:, g], pv[:, g % 2, 16:], start=True, stop=True) \
                            .then_inc(pool_mixed, 1)
                    if n >= 4:
                        outputs(n - 4)
                for q in range(4):
                    c = T_GLU + q
                    pe.wait_ge(w_split, c + 1)
                    for m in range(2):
                        for k in range(4):
                            if q == 0:
                                pe.wait_ge(yl_ready, k + 1)
                            bank = ps[[4, 6, 0, 2][q] + m][:]
                            pe.matmul(bank, w_hi[:, c % RING, 2 * k + m], h_hi[:, k], start=(k == 0), stop=False)
                            pe.matmul(bank, w_hi[:, c % RING, 2 * k + m], h_lo[:, k], start=False, stop=False)
                            mm = pe.matmul(bank, w_lo[:, c % RING, 2 * k + m], h_hi[:, k], start=False, stop=(k == 3))
                    mm.then_inc(w_used, 1)

            def odd_mixer():
                def mean(t):
                    pe.wait_ge(cv_ready, t + 1)
                    pe.matmul(ps[6][:], ones[:], cv[:, t], start=(t == 0), stop=(t == KT - 1)).then_inc(mean_sum, 1)

                pe.wait_ge(cw_in, 16)
                for t in range(KT):
                    mm = pe.transpose(ps[5][:, t * 32:t * 32 + TAPS], cw_rows[:, t * P:(t + 1) * P],
                                      ident[0:TAPS, 0:TAPS])
                mm.then_inc(cw_t, 1)
                for n in range(3 * KT):
                    if n == 0:
                        pe.wait_ge(rs_ready, N_ODD + 1)
                    upto(pe, odd_read, n - 3 - (n - 1) // 3)
                    upto(pe, g_ready, (n - 4 + 2) // 3)
                    project(0, T_ODD + n, n % 4, 4 * KT if n == 0 else None)
                    if n % 3 == 2 and n > 6:
                        mean(n // 3 - 2)
                mean(KT - 2)
                mean(KT - 1)
                for t in range(KT):
                    pe.wait_ge(cq_ready, t + 1)
                    pe.matmul(ps[7][:], ones[:], sq[:, t % 2], start=(t == 0), stop=(t == KT - 1)).then_inc(var_sum, 1)

            def project_out_by_rows(t0, mixed, norm_after):
                for j in range(KT - 3):
                    pe.wait_ge(w_split, t0 + j + 1)
                    pe.wait_ge(mix_ready, mixed + j + 1)
                    for n in range(KT):
                        mm = three(ps[n][:], (t0 + j) % RING, n, a_hi[:, j * S:(j + 1) * S],
                                   a_lo[:, j * S:(j + 1) * S], j == 0, False)
                    mm.then_inc(w_used, 1)
                pe.wait_ge(w_split, t0 + KT)
                pe.wait_ge(mix_ready, mixed + KT)
                for n in range(KT):
                    for j in range(KT - 3, KT):
                        mm = three(ps[n][:], (t0 + j) % RING, n, a_hi[:, j * S:(j + 1) * S],
                                   a_lo[:, j * S:(j + 1) * S], False, j == KT - 1)
                        if n == KT - 1:
                            mm.then_inc(w_used, 1)
                    if n < KT - 1:
                        mm.then_inc(out_done, 1)
                    if n >= 2:
                        norm_sum(norm_after, n - 2)
                norm_sum(norm_after, KT - 2)
                norm_sum(norm_after, KT - 1)

            project_in()
            mlstm()
            attention()
            project_out(T_OUT, 0, X_MIX, 2)
            ffn(1, 2, N_FIN, False, set_up)
            for kt in range(KT):
                if kt == 0:
                    pe.wait_ge(rs_ready, N_FIN + 1)
                norm_sum(N_EVEN, kt)
            even_mixer()
            pe.wait_ge(glu_read, 2)
            project_out(T_EOUT, KT, X_EVEN, N_ODD, 4)
            odd_mixer()
            project_out_by_rows(T_OOUT, 2 * KT, N_LAST)
            for kt in range(KT):
                pe.wait_ge(fin_ready, kt + 1)
                for st in range(ST):
                    mm = pe.transpose(ps[2 * st + kt // 4][:, kt % 4 * P:(kt % 4 + 1) * P],
                                      xT[:, kt, st * P:(st + 1) * P], ident[:])
                mm.then_inc(out_t, 1)


_INS = ["x", "c", "w_ada", "b_ada", "g_ffn1", "w_gu1", "w_down1", "g_mix", "w_in", "gate_bias", "g_q", "g_k", "g_mh",
        "w_out", "g_ffn2", "w_gu2", "w_down2", "g_final", "even_norm_2", "even_w_in_2", "pool_w_2", "pool_scale_2",
        "ssm_log_dt_2", "ssm_a_re_2", "ssm_a_im_2", "ssm_b_re_2", "ssm_b_im_2", "ssm_c_re_2", "ssm_c_im_2", "ssm_d_2",
        "ssm_w_glu_2", "even_w_out_2", "odd_norm_2", "odd_w_in_2", "conv_w_2", "conv_b_2", "conv_ln_g_2",
        "conv_ln_b_2", "odd_w_out_2", "final_norm_2"]


def kernel(**inputs):
    import concourse.bacc as _bacc
    from concourse.bass_utils import run_bass_kernel_spmd

    nc = _bacc.Bacc("TRN2", target_bir_lowering=False, num_devices=1)
    arrays, a = {}, {}
    for name, value in [(name, inputs[name]) for name in _INS] + list(constants().items()):
        value = np.ascontiguousarray(value)
        arrays[f"in_{name}"] = value
        a[name] = nc.dram_tensor(f"in_{name}", value.shape, mybir.dt.from_np(value.dtype), kind="ExternalInput").ap()
    out = nc.dram_tensor("out", (1, S, D), F32, kind="ExternalOutput").ap()
    build_program(nc, a, out[0])
    results = run_bass_kernel_spmd(nc, [arrays], core_ids=[0])
    return results.results[0]["out"]
```
